# Optimizing a Trainium2 kernel written in Bass

```python
import math
import jax
import jax.numpy as jnp
from jax import lax
import numpy as np

D_MODEL = 2048
BATCH = 1
SEQ = 256
DEPTH = 2

HEAD_DIM = 128
N_HEADS = D_MODEL // HEAD_DIM
BLOCK = 128
GRID_W = 64
ROW_WIN = 8
COL_WIN = 16
A_HEADS = N_HEADS // 2
B_HEADS = N_HEADS // 2
DIFF_QK_DIM = HEAD_DIM // 2
LAMBDA_INIT = 0.2
C_HEADS = N_HEADS // 2
C_PATTERNS = ((128, 1), (512, 4), (2048, 16))
C_GROUPS = len(C_PATTERNS)
D_HEADS = N_HEADS // 2
D_KV_HEADS = D_HEADS // 4
D_HALF_WINDOW = 128
ROPE_THETA = 500000.0
ROPE_FRACTION = 4
RMS_EPS = 1e-6
NEG_INF = -1e30

EVEN_IN_WIDTHS = (
    A_HEADS * HEAD_DIM, A_HEADS * HEAD_DIM, A_HEADS * HEAD_DIM, A_HEADS * HEAD_DIM,
    B_HEADS * 2 * DIFF_QK_DIM, B_HEADS * 2 * DIFF_QK_DIM, B_HEADS * HEAD_DIM, B_HEADS * HEAD_DIM,
)
EVEN_OUT = A_HEADS * HEAD_DIM + B_HEADS * HEAD_DIM
ODD_IN_WIDTHS = (
    C_GROUPS * C_HEADS * HEAD_DIM, C_GROUPS * C_HEADS * HEAD_DIM, C_GROUPS * C_HEADS * HEAD_DIM, C_HEADS * HEAD_DIM,
    D_HEADS * HEAD_DIM, D_KV_HEADS * HEAD_DIM, D_KV_HEADS * HEAD_DIM, D_HEADS * HEAD_DIM,
)
ODD_OUT = C_HEADS * HEAD_DIM + D_HEADS * HEAD_DIM

kernel_name = "hybrid_natten_diff_dilated_swa_encoder"

def rms_norm(x, g):
    xf = x.astype(jnp.float32)
    y = xf * lax.rsqrt(jnp.mean(xf * xf, axis=-1, keepdims=True) + RMS_EPS)
    return y.astype(x.dtype) * g

def _split(t, widths):
    out, start = [], 0
    for w in widths:
        out.append(t[..., start:start + w])
        start += w
    return out

def partial_rope(x, pos):
    dh = x.shape[-1]
    rd = dh // ROPE_FRACTION
    half = rd // 2
    inv = ROPE_THETA ** (-jnp.arange(half, dtype=jnp.float32) / half)
    ang = pos.astype(jnp.float32)[:, None] * inv[None, :]
    shape = (1, x.shape[1]) + (1,) * (x.ndim - 3) + (half,)
    cos = jnp.cos(ang).reshape(shape)
    sin = jnp.sin(ang).reshape(shape)
    xr = x[..., :rd].astype(jnp.float32)
    x1, x2 = xr[..., :half], xr[..., half:]
    rot = jnp.concatenate([x1 * cos - x2 * sin, x2 * cos + x1 * sin], axis=-1)
    return jnp.concatenate([rot.astype(x.dtype), x[..., rd:]], axis=-1)

def neighbourhood_attention(q, k, v, rpb):
    b, s, h, dh = q.shape
    rows = s // GRID_W
    wr = min(ROW_WIN, rows)
    r = jnp.arange(rows)
    row_start = jnp.clip(r - ROW_WIN // 2, 0, rows - wr)
    row_idx = row_start[:, None] + jnp.arange(wr)[None, :]
    qg = q.reshape(b, rows, GRID_W, h, dh)
    kg = k.reshape(b, rows, GRID_W, h, dh)[:, row_idx]
    vg = v.reshape(b, rows, GRID_W, h, dh)[:, row_idx]
    sc = jnp.einsum("brchd,brjkhd->brhcjk", qg, kg).astype(jnp.float32) * (dh ** -0.5)
    c = jnp.arange(GRID_W)
    col_start = jnp.clip(c - COL_WIN // 2, 0, GRID_W - COL_WIN)
    col_ok = (c[None, :] >= col_start[:, None]) & (c[None, :] < col_start[:, None] + COL_WIN)
    dr_i = row_idx - r[:, None] + ROW_WIN - 1
    dc_i = jnp.clip(c[None, :] - c[:, None] + COL_WIN - 1, 0, 2 * COL_WIN - 2)
    bias = rpb[:, dr_i][:, :, :, dc_i]
    bias = bias.transpose(1, 0, 3, 2, 4).astype(jnp.float32)
    sc = jnp.where(col_ok[:, None, :], sc + bias[None], NEG_INF)
    p = jax.nn.softmax(sc, axis=(-2, -1))
    o = jnp.einsum("brhcjk,brjkhd->brchd", p.astype(v.dtype), vg)
    return o.reshape(b, s, h, dh)

def diff_attention(q, k, v, lam):
    b, s, h, _, dq = q.shape
    dv = v.shape[-1]
    nb = s // BLOCK
    qb = jnp.moveaxis(q.reshape(b, nb, BLOCK, h, 2, dq), 1, 0)

    def one_block(qblk):
        sc = jnp.einsum("bqhcd,bkhcd->bchqk", qblk, k).astype(jnp.float32) * (dq ** -0.5)
        p = jax.nn.softmax(sc, axis=-1)
        a = p[:, 0] - lam * p[:, 1]
        return jnp.einsum("bhqk,bkhd->bqhd", a.astype(v.dtype), v)

    o = lax.map(one_block, qb)
    return jnp.moveaxis(o, 0, 1).reshape(b, s, h, dv)

def banded_attention(q, k, v, half):
    n, L, hk, g, dh = q.shape
    nb = -(-L // BLOCK)
    lp = nb * BLOCK
    kb = BLOCK + 2 * half
    qp = jnp.pad(q, ((0, 0), (0, lp - L), (0, 0), (0, 0), (0, 0)))
    pad_kv = ((0, 0), (half, lp - L + half), (0, 0), (0, 0))
    kp = jnp.pad(k, pad_kv)
    vp = jnp.pad(v, pad_kv)
    blk = jnp.arange(nb)[:, None] * BLOCK
    key_idx = blk + jnp.arange(kb)[None, :]
    k_blk = kp[:, key_idx]
    v_blk = vp[:, key_idx]
    q_blk = qp.reshape(n, nb, BLOCK, hk, g, dh)
    sc = jnp.einsum("nbqhgd,nbkhd->nbhgqk", q_blk, k_blk).astype(jnp.float32) * (dh ** -0.5)
    q_pos = blk + jnp.arange(BLOCK)[None, :]
    k_pos = key_idx - half
    valid = ((jnp.abs(q_pos[:, :, None] - k_pos[:, None, :]) <= half)
             & ((k_pos >= 0) & (k_pos < L))[:, None, :])
    sc = jnp.where(valid[None, :, None, None], sc, NEG_INF)
    lse = jax.nn.logsumexp(sc, axis=-1)
    p = jnp.exp(sc - lse[..., None])
    o = jnp.einsum("nbhgqk,nbkhd->nbqhgd", p.astype(v.dtype), v_blk)
    o = o.reshape(n, lp, hk, g, dh)[:, :L]
    lse = lse.transpose(0, 1, 4, 2, 3).reshape(n, lp, hk, g)[:, :L]
    return o, lse

def _fold(t, dil):
    b, s = t.shape[:2]
    rest = t.shape[2:]
    return t.reshape((b, s // dil, dil) + rest).swapaxes(1, 2).reshape((b * dil, s // dil) + rest)

def _unfold(t, b, dil):
    n, l = t.shape[:2]
    rest = t.shape[2:]
    return t.reshape((b, dil, l) + rest).swapaxes(1, 2).reshape((b, l * dil) + rest)

def dilated_mixture_attention(q, k, v):
    b = q.shape[0]
    outs, lses = [], []
    for gi, (window, dil) in enumerate(C_PATTERNS):
        half = (window // 2) // dil
        o, lse = banded_attention(_fold(q[:, :, gi], dil)[:, :, :, None],
                                  _fold(k[:, :, gi], dil), _fold(v[:, :, gi], dil), half)
        outs.append(_unfold(o[:, :, :, 0], b, dil))
        lses.append(_unfold(lse[:, :, :, 0], b, dil))
    w = jax.nn.softmax(jnp.stack(lses, axis=0), axis=0)
    o = jnp.stack(outs, axis=0)
    return jnp.sum(w[..., None].astype(o.dtype) * o, axis=0)

def even_layer(x, pre_g, w_in, rpb, lam_q1, lam_k1, lam_q2, lam_k2, subln_g, w_out, post_g):
    b, s, _ = x.shape
    pos = jnp.arange(s)
    h = rms_norm(x, pre_g)
    qa, ka, va, ga, qb, kb, vb, gb = _split(h @ w_in, EVEN_IN_WIDTHS)
    oa = neighbourhood_attention(qa.reshape(b, s, A_HEADS, HEAD_DIM), ka.reshape(b, s, A_HEADS, HEAD_DIM),
                                 va.reshape(b, s, A_HEADS, HEAD_DIM), rpb)
    qb = partial_rope(qb.reshape(b, s, B_HEADS, 2, DIFF_QK_DIM), pos)
    kb = partial_rope(kb.reshape(b, s, B_HEADS, 2, DIFF_QK_DIM), pos)
    lam = (jnp.exp(jnp.sum(lam_q1.astype(jnp.float32) * lam_k1.astype(jnp.float32)))
           - jnp.exp(jnp.sum(lam_q2.astype(jnp.float32) * lam_k2.astype(jnp.float32))) + LAMBDA_INIT)
    ob = diff_attention(qb, kb, vb.reshape(b, s, B_HEADS, HEAD_DIM), lam)
    ob = rms_norm(ob, subln_g) * (1.0 - LAMBDA_INIT)
    mix = jnp.concatenate([oa.reshape(b, s, -1) * jax.nn.silu(ga),
                           ob.reshape(b, s, -1) * jax.nn.silu(gb)], axis=-1)
    return x + rms_norm(mix @ w_out, post_g)

def odd_layer(x, pre_g, w_in, sink, w_out, post_g):
    b, s, _ = x.shape
    pos = jnp.arange(s)
    h = rms_norm(x, pre_g)
    qc, kc, vc, gc, qd, kd, vd, gd = _split(h @ w_in, ODD_IN_WIDTHS)
    qc = partial_rope(qc.reshape(b, s, C_GROUPS, C_HEADS, HEAD_DIM), pos)
    kc = partial_rope(kc.reshape(b, s, C_GROUPS, C_HEADS, HEAD_DIM), pos)
    oc = dilated_mixture_attention(qc, kc, vc.reshape(b, s, C_GROUPS, C_HEADS, HEAD_DIM))
    grp = D_HEADS // D_KV_HEADS
    qd = partial_rope(qd.reshape(b, s, D_HEADS, HEAD_DIM), pos).reshape(b, s, D_KV_HEADS, grp, HEAD_DIM)
    kd = partial_rope(kd.reshape(b, s, D_KV_HEADS, HEAD_DIM), pos)
    od, lse = banded_attention(qd, kd, vd.reshape(b, s, D_KV_HEADS, HEAD_DIM), D_HALF_WINDOW)
    sink_f = sink.astype(jnp.float32).reshape(D_KV_HEADS, grp)
    od = od * jnp.exp(lse - jnp.logaddexp(lse, sink_f))[..., None].astype(od.dtype)
    mix = jnp.concatenate([oc.reshape(b, s, -1) * jax.nn.silu(gc),
                           od.reshape(b, s, -1) * jax.nn.silu(gd)], axis=-1)
    return x + rms_norm(mix @ w_out, post_g)

def setup_inputs(seed: int = 0) -> dict:
    key = jax.random.key(seed)
    ks = jax.random.split(key, 16)
    d = D_MODEL

    def nrm(k, shape, scale):
        return jax.random.normal(k, shape, jnp.float32) * scale

    even_in = sum(EVEN_IN_WIDTHS)
    odd_in = sum(ODD_IN_WIDTHS)
    return {
        "x": nrm(ks[0], (BATCH, SEQ, D_MODEL), 1.0),
        "l0_pre_g": 1.0 + nrm(ks[1], (d,), 0.05),
        "l0_w_in": nrm(ks[2], (d, even_in), d ** -0.5),
        "l0_rpb": nrm(ks[3], (A_HEADS, 2 * ROW_WIN - 1, 2 * COL_WIN - 1), 0.5),
        "l0_lam_q1": nrm(ks[4], (DIFF_QK_DIM,), 0.1),
        "l0_lam_k1": nrm(ks[5], (DIFF_QK_DIM,), 0.1),
        "l0_lam_q2": nrm(ks[6], (DIFF_QK_DIM,), 0.1),
        "l0_lam_k2": nrm(ks[7], (DIFF_QK_DIM,), 0.1),
        "l0_subln_g": 1.0 + nrm(ks[8], (HEAD_DIM,), 0.05),
        "l0_w_out": nrm(ks[9], (EVEN_OUT, d), EVEN_OUT ** -0.5),
        "l0_post_g": 1.0 + nrm(ks[10], (d,), 0.05),
        "l1_pre_g": 1.0 + nrm(ks[11], (d,), 0.05),
        "l1_w_in": nrm(ks[12], (d, odd_in), d ** -0.5),
        "l1_sink": nrm(ks[13], (D_HEADS,), 1.0),
        "l1_w_out": nrm(ks[14], (ODD_OUT, d), ODD_OUT ** -0.5),
        "l1_post_g": 1.0 + nrm(ks[15], (d,), 0.05),
    }

def reference(x, l0_pre_g, l0_w_in, l0_rpb, l0_lam_q1, l0_lam_k1, l0_lam_q2, l0_lam_k2,
              l0_subln_g, l0_w_out, l0_post_g, l1_pre_g, l1_w_in, l1_sink, l1_w_out, l1_post_g):
    layer_params = (
        (l0_pre_g, l0_w_in, l0_rpb, l0_lam_q1, l0_lam_k1, l0_lam_q2, l0_lam_k2, l0_subln_g, l0_w_out, l0_post_g),
        (l1_pre_g, l1_w_in, l1_sink, l1_w_out, l1_post_g),
    )
    for layer in range(DEPTH):
        if layer % 2 == 0:
            x = even_layer(x, *layer_params[layer])
        else:
            x = odd_layer(x, *layer_params[layer])
    return x


_drawn_inputs = setup_inputs


def setup_inputs(seed=0):
    import zlib

    import numpy as np

    out = dict(_drawn_inputs(seed))
    spreads = {}
    factors = {'l1_sink': 8.0}
    for name, (base, spread) in spreads.items():
        noise = np.random.default_rng([zlib.crc32(name.encode()), seed]).standard_normal(out[name].shape)
        drawn = base * np.exp(spread * noise) if base else spread * noise
        out[name] = jnp.asarray(drawn.astype(out[name].dtype))
    for name, factor in factors.items():
        out[name] = (out[name] * factor).astype(out[name].dtype)
    return out
```

```python
from contextlib import ExitStack
import math

import numpy as np
import concourse.bass as bass
from concourse import mybir

ALU = mybir.AluOpType
ACT = mybir.ActivationFunctionType
AX_X = mybir.AxisListType.X
F32 = mybir.dt.float32
F32R = mybir.dt.float32r

P = 128
SEQ = 256
D_MODEL = 2048
NT = SEQ // P
KT = D_MODEL // P
NB = 512
CK = 4
CHUNKS = KT // CK
HEAD = 128
UH = NB // HEAD
BODY = 3 * CHUNKS
RAW = 4
SPLIT = 3
NEG = -1.0e30
EPS = 1e-6
OUT_BLOCKS = D_MODEL // NB
GRID_W = 64
ROWS = SEQ // GRID_W
RPB_R, RPB_C = 15, 31
SCALE = HEAD ** -0.5
SCALE_B = (HEAD // 2) ** -0.5
LAMBDA_INIT = 0.2

CREDIT = 1
CREDITED = ("o_full", "o_taken", "pt_full", "pt_ready", "probs_ready", "unit_done", "o_squared", "roped")

BODIES = (5, 8)
LAYER_CHUNKS = [n * BODY + CHUNKS + OUT_BLOCKS * CHUNKS for n in BODIES]
CHUNK0 = (0, LAYER_CHUNKS[0])
ALL_CHUNKS = sum(LAYER_CHUNKS)
OUT_ORDER = ([(0, c) for c in range(3)] + [(1, c) for c in range(3)] + [(0, 3), (1, 3)]
             + [(2, c) for c in range(4)] + [(3, c) for c in range(4)])
OUT_SET = (1, 2, 0, 1)
GATE_SLOTS = (0, 1, 2, 4)
TURN_SLOTS = (1, 2, 3, 5)
OUT_SLOTS = tuple(CHUNKS + OUT_ORDER.index((n, 3)) + 1 for n in range(OUT_BLOCKS))
HEADS = (16, 48)
UNITS = (4, 11)
PROJ0 = (0, 3 * BODIES[0] + 1)

CONST_COLS = {}
_at = 0
for _name, _n in (("ident", P), ("mask_a", SEQ), ("mask_w", NT * SEQ), ("mask_g1", P), ("mask_g2", P),
                  ("mask_d", NT * SEQ), ("cos0", 256), ("sin0", 256), ("cos1", 256), ("sin1", 256)):
    CONST_COLS[_name] = (_at, _n)
    _at += _n
CONST_N = _at


class Unit:

    def __init__(self, kind, layer, body, index, step=0, mask=None):
        self.kind, self.layer, self.mask = kind, layer, mask
        self.step = step
        self.body = body + step
        self.index = index + step
        self.heads = 8 if kind == "D" else UH

    def head(self, j):
        return CREDIT + UH * self.index + j

    def plain(self, j):
        return UH * self.index + j - (2 * UH if self.layer else 0)

    def diff(self, j):
        return UH * self.index + j - 2 * UH

    def at(self, j):
        return 5 + 2 * j if self.kind == "D" else 6 + 4 * j

    def stages(self, h, *offsets):
        return [j for j in range(self.heads) if h - self.at(j) in offsets]


ATTENTION = [
    ("A", 0, 1, 0, 2, None), ("B", 0, 3, 2, 2, None),
    ("W", 1, 1, 4, 2, "mask_w"), ("G", 1, 3, 6, 2, "mask_g1"), ("G", 1, 5, 8, 2, "mask_g2"),
    ("D", 1, 7, 10, 1, "mask_d"),
]


def build(nc, weights, x_nat, x_perm, consts, pre_g, post_g, rpb, lam, subln, sink, out):
    with ExitStack() as ctx:
        def sb(name, shape, dt=F32):
            return ctx.enter_context(nc.sbuf_tensor(name, shape, dt))

        def sem(name):
            return ctx.enter_context(nc.semaphore(name))

        credit = sb("credit", [P, len(CREDITED)])
        raw = sb("raw", [P, RAW, CK * NB])
        w_hi = sb("w_hi", [P, SPLIT, CK * NB], F32R)
        w_lo = sb("w_lo", [P, SPLIT, CK * NB], F32R)
        act_hi = sb("act_hi", [P, KT, SEQ], F32R)
        act_lo = sb("act_lo", [P, KT, SEQ], F32R)
        unit = sb("unit", [P, 3, NT, NB])
        mix = sb("mix", [P, NT, D_MODEL])
        resid = sb("resid", [P, NT, D_MODEL])
        qT = sb("qT", [P, UH * SEQ])
        kT = sb("kT", [P, UH * SEQ])
        scores = sb("scores", [P, 2, NT * SEQ])
        probs = sb("probs", [P, 2, NT * SEQ])
        pT = sb("pT", [P, 2 * SEQ])
        unit_out = sb("unit_out", [P, NT, NB])
        cst = sb("cst", [P, CONST_N])
        postg = sb("postg", [P, D_MODEL])
        preg = sb("preg", [P, 2, KT])
        rope_c = sb("rope_c", [P, 256])
        rope_s = sb("rope_s", [P, 256])
        lamv = sb("lamv", [P, 4, 64])
        lamp = sb("lamp", [P, 2, 64])
        lams = sb("lams", [P, 2])
        lame = sb("lame", [P, 2])
        neglam = sb("neglam", [P, 1])
        subg = sb("subg", [P, NT, HEAD])
        sinkb = sb("sinkb", [P, 8])
        negsink = sb("negsink", [P, 8])
        sqo = sb("sqo", [P, NB])
        pre_ss = sb("pre_ss", [P, NT, 4])
        y_ss = sb("y_ss", [P, NT, OUT_BLOCKS])
        ss = sb("ss", [P, NT])
        var = sb("var", [P, NT])
        std = sb("std", [P, NT])
        pre_r = sb("pre_r", [P, NT])
        post_r = sb("post_r", [P, NT])
        rmax = sb("rmax", [P, 16])
        negm = sb("negm", [P, 16])
        usum = sb("usum", [P, 16])
        sinke = sb("sinke", [P, 16])
        bmax = sb("bmax", [P, 2, NT])
        bneg = sb("bneg", [P, 2, NT])
        bsum = sb("bsum", [P, 2, NT])
        binv = sb("binv", [P, 2, NT])
        bw = sb("bw", [P, NT])
        cneg = sb("cneg", [P, 2, 8])
        newneg = sb("newneg", [P, 8])
        dexp = sb("dexp", [P, 2, 8])
        wexp = sb("wexp", [P, 2, 8])
        wsum = sb("wsum", [P, 8])
        row_sum = sb("row_sum", [P, 32])
        row_scale = sb("row_scale", [P, 32])
        bstd = sb("bstd", [P, 16])
        bias_in = mix[:, :, :].rearrange("p t n -> p (t n)")
        bias_a = resid[:, :, :].rearrange("p t n -> p (t n)")
        scores_flat = scores[:, :, :].rearrange("p a n -> p (a n)")
        probs_flat = probs[:, :, :].rearrange("p a n -> p (a n)")
        unit_out_flat = unit_out[:, :, :].rearrange("p t n -> p (t n)")

        acc = [[ctx.enter_context(nc.psum_tensor(f"acc{s}_{t}", [P, NB], F32)) for t in range(NT)]
               for s in range(3)]
        bank = [ctx.enter_context(nc.psum_tensor(f"bank_{n}", [P, NB], F32)) for n in ("x", "y")]
        X, Y = bank

        names = ("consts_in x_in bias_in vecs_in resid_in postg_in out_sent "
                 "hi_ready lo_ready chunk_used proj_ready roped rope_a "
                 "turn_full turn_hi turn_taken qk_full qk_ready "
                 "s_full masked maxed negm_ready probs_ready sink_ready "
                 "map0_full map1_full map0_max map1_max map0_neg map1_neg map0_exp map1_exp b_inv b_w b_scaled "
                 "pt_full pt_ready o_full o_squared o_taken unit_done "
                 "m_new m_diff m_exp m_wsum m_rsum m_old m_scaled "
                 "pre_sq pre_sum pre_var pre_std pre_rdy lam_p lam_s lam_e lam_rdy bias_rdy negsink_rdy "
                 "y_sq y_scaled y_part y_sum y_var y_std y_rdy x_new "
                 "rs_v rs_s rs_rdy tanh_done gate_u gate_done").split()
        S = {n: sem(n) for n in names}
        landed = [sem(f"landed{i}") for i in range(RAW)]

        def const(name):
            a, n = CONST_COLS[name]
            return cst[:, a:a + n]

        ident = const("ident")

        def loops(eng, layer):
            yield None, 0, 0
            for kind, lay, body, index, count, mask in ATTENTION:
                if lay != layer:
                    continue
                if count == 1:
                    yield Unit(kind, lay, body, index, 0, mask), body, 0
                else:
                    with eng.Fori(0, count) as i:
                        yield Unit(kind, lay, body, index, i, mask), body, i

        block = ctx.enter_context(nc.Block())

        @block.sync
        def _(sp):
            for g in range(RAW):
                sp.dma_start(raw[:, g, :], weights[g]).then_inc(landed[g], 16)
            with sp.Fori(1, ALL_CHUNKS // RAW) as n:
                src = [sp.snap(n * RAW + r) for r in range(RAW)]
                free = [sp.snap(n * RAW + r - RAW + 1) for r in range(RAW)]
                for r in range(RAW):
                    sp.wait_ge(S["lo_ready"], free[r])
                    sp.dma_start(raw[:, r, :], weights[bass.ds(src[r], 1)].rearrange("a p n -> p (a n)")).then_inc(
                        landed[r], 16)
            for n in range(OUT_BLOCKS):
                cols = slice(n * NB, (n + 1) * NB)
                sp.wait_ge(S["x_new"], NT * (OUT_BLOCKS + n + 1))
                sp.dma_start(out[:, cols].rearrange("(t p) n -> p t n", p=P), resid[:, :, cols]).then_inc(S["out_sent"], 16)
            sp.wait_ge(S["out_sent"], 16 * OUT_BLOCKS)

        @block.gpsimd
        def _(pool):
            for n, name in enumerate(CREDITED):
                pool.memset(credit[:, n:n + 1], 0.0).then_inc(S[name], CREDIT)
            for t in range(NT):
                pool.dma_start(resid[:, t, :], x_nat[t * P:(t + 1) * P, :]).then_inc(S["x_in"], 16)
            pool.dma_start(cst[:, :], consts).then_inc(S["consts_in"], 16)
            pool.dma_start(preg[:, :, :], pre_g).then_inc(S["vecs_in"], 16)
            pool.dma_start(lamv[:, :, :].rearrange("p a b -> p (a b)"), lam.partition_broadcast(P)).then_inc(S["vecs_in"], 16)
            for t in range(NT):
                pool.dma_start(subg[:, t, :], subln.partition_broadcast(P)).then_inc(S["vecs_in"], 16)
            pool.dma_start(sinkb[:, :], sink.partition_broadcast(P)).then_inc(S["vecs_in"], 16)
            for t in range(NT):
                for half in range(2):
                    r = 2 * t + half
                    for h in range(8):
                        src = bass.AP(rpb.tensor, h * RPB_R * RPB_C + (7 - r) * RPB_C + 15 - (GRID_W - 1),
                                      [[1, GRID_W], [RPB_C, ROWS], [1, GRID_W]])
                        at = (h * NT + t) * SEQ
                        pool.dma_start(bias_in[half * 64:half * 64 + 64, at:at + SEQ].rearrange(
                            "p (j k) -> p j k", j=ROWS), src).then_inc(S["bias_in"], 16)
            pool.dma_start(postg[:, :], post_g[0].partition_broadcast(P)).then_inc(S["postg_in"], 16)

            def rotate(u, k, blk, cols, group):
                width = group // 4
                n_groups = NT * cols // group
                if cols == NB:
                    v = unit[:, blk, :, :].rearrange("p t (g c) -> p (t g) c", c=group)
                    view = lambda a: a.rearrange("p (g c) -> p g c", c=width)
                else:
                    v = unit[:, blk, :, 0:cols].rearrange("p t (g c) -> p t g c", c=group)
                    view = lambda a: a.rearrange("p (t g c) -> p t g c", t=NT, c=width)
                n = n_groups * width
                cos, sin = const(f"cos{u.layer}"), const(f"sin{u.layer}")
                if cols != NB:
                    sl = lambda a: a.rearrange("p (t g c) -> p t g c", t=NT, c=width)[:, :, 0:cols // group, :]
                    cos, sin = sl(cos), sl(sin)
                else:
                    cos, sin = view(cos), view(sin)
                rc, rs = view(rope_c[:, 0:n]), view(rope_s[:, 0:n])
                h = width // 2
                idx = (slice(None),) * (2 if cols == NB else 3)
                first, second, whole = idx + (slice(0, h),), idx + (slice(h, width),), idx + (slice(0, width),)
                count = 2 * (u.index - 2) + k
                pool.tensor_tensor(rc, v[whole], cos, ALU.mult).then_inc(S["rope_a"], 1)
                pool.tensor_tensor(rs[first], v[second], sin[first], ALU.mult).then_inc(S["rope_a"], 1)
                pool.tensor_tensor(rs[second], v[first], sin[second], ALU.mult).then_inc(S["rope_a"], 1)
                pool.wait_ge(S["rope_a"], 3 * count + 3)
                pool.tensor_tensor(v[whole], rc, rs, ALU.add).then_inc(S["roped"], 1)

            pool.wait_ge(S["consts_in"], 16)
            for layer in range(2):
                for u, _, _ in loops(pool, layer):
                    if u is None or u.kind == "A":
                        continue
                    turns = ((0, NB), (1, NB), (2, 2 * HEAD)) if u.kind == "D" else ((0, NB), (1, NB))
                    for k, (blk, cols) in enumerate(turns):
                        pool.wait_ge(S["proj_ready"], PROJ0[layer] + 3 * u.body - 2 + k)
                        pool.wait_ge(S["roped"], CREDIT + 2 * (u.index - 2) + k)
                        rotate(u, k, blk, cols, HEAD // 2 if layer == 0 else HEAD)
                if layer == 0:
                    pool.wait_ge(S["masked"], 2 * UH)
                    for t in range(NT):
                        pool.dma_start(resid[:, t, :], x_perm[t * P:(t + 1) * P, :]).then_inc(S["resid_in"], 16)
                    pool.wait_ge(S["y_scaled"], OUT_BLOCKS)
                    pool.dma_start(postg[:, :], post_g[1].partition_broadcast(P)).then_inc(S["postg_in"], 16)

        @block.tensor
        def _(pe):
            def half_chunk(g, buf, half, tiles, first):
                if half == 0:
                    pe.wait_ge(S["lo_ready"], g + 1)
                for kk in (2 * half, 2 * half + 1):
                    kt = first + kk
                    for t in range(NT):
                        sl = slice(t * P, (t + 1) * P)
                        cols = slice(kk * NB, (kk + 1) * NB)
                        for n, (a, w) in enumerate(((act_hi, w_hi), (act_hi, w_lo), (act_lo, w_hi))):
                            m = nc.tensor.matmul(tiles[t][:, :], a[:, kt, sl], w[:, buf, cols],
                                                 start=(kt == 0 and n == 0), stop=(kt == KT - 1 and n == 2))
                if half == 1:
                    m.then_inc(S["chunk_used"], 1)

            def turn(f, srcs):
                if f >= 2:
                    pe.wait_ge(S["turn_taken"], f - 1)
                for n, src in enumerate(srcs):
                    m = nc.tensor.transpose(bank[f % 2][:, n * P:(n + 1) * P], src, ident)
                m.then_inc(S["turn_full"], 1)

            def turn_x(layer, k):
                if layer == 1:
                    if k % 2 == 0:
                        pe.wait_ge(S["x_new"], 2 * (k // 2 + 1))
                turn(16 * layer + k, [resid[:, t, kt * P:(kt + 1) * P] for kt in (2 * k, 2 * k + 1) for t in range(NT)])

            def turn_mix(layer, c, f):
                if f == 0:
                    pe.wait_ge(S["gate_done"], 4 * layer + c + 1)
                k = 2 * c + f
                turn(16 * layer + 8 + k,
                     [mix[:, t, kt * P:(kt + 1) * P] for kt in (2 * k, 2 * k + 1) for t in range(NT)])

            def qk_fills(u, fills):
                for f in fills:
                    if u.kind == "D":
                        blk, h0 = ((0, 0), (0, 2), (1, 0), (1, 2), (2, 0))[f]
                        need = (1, 1, 2, 2, 3)[f]
                    else:
                        blk, h0 = ((0, 0), (0, 2), (1, 0), (1, 2))[f]
                        need = (1, 1, 2, 2)[f]
                    if f == 0:
                        pe.wait_ge(S["turn_taken"], 16 * u.layer + 8)
                        pe.wait_ge(S["o_taken"], u.head(0))
                    if f >= 2:
                        pe.wait_ge(S["qk_ready"], 4 * u.index + f - 1)
                    if u.kind == "A":
                        pe.wait_ge(S["proj_ready"], PROJ0[0] + 3 * (u.body - 1) + need)
                    else:
                        pe.wait_ge(S["roped"], CREDIT + 2 * (u.index - 2) + need)
                    for n, (h, t) in enumerate(((h0, 0), (h0, 1), (h0 + 1, 0), (h0 + 1, 1))):
                        m = nc.tensor.transpose(bank[f % 2][:, n * P:(n + 1) * P],
                                                unit[:, blk, t, h * HEAD:(h + 1) * HEAD], ident)
                    m.then_inc(S["qk_full"], 1)

            def score(u, j):
                q = qT[:, :] if j < UH else unit_out_flat
                jq, jk = j % UH, (j // UH if u.kind == "D" else j)
                pe.wait_ge(S["qk_ready"], 4 * u.index + (5 if u.kind == "D" else 4))
                if j > 0:
                    pe.wait_ge(S["masked"], u.plain(j))
                for t in range(NT):
                    lhs = q[:, jq * SEQ + t * P:jq * SEQ + (t + 1) * P]
                    if u.kind == "G":
                        m = nc.tensor.matmul(Y[:, t * P:(t + 1) * P], lhs,
                                             kT[:, jk * SEQ + t * P:jk * SEQ + (t + 1) * P], start=True, stop=True)
                    else:
                        m = nc.tensor.matmul(Y[:, t * SEQ:(t + 1) * SEQ], lhs,
                                             kT[:, jk * SEQ:(jk + 1) * SEQ], start=True, stop=True)
                m.then_inc(S["s_full"], 1)

            def score_map(u, j, c):
                if c == 0:
                    pe.wait_ge(S["qk_ready"], 4 * u.index + 4)
                    if j > 0:
                        pe.wait_ge(S["map0_exp"], u.diff(j))
                else:
                    if j > 0:
                        pe.wait_ge(S["o_taken"], u.head(j))
                rows = slice(64 * c, 64 * c + 64)
                for t in range(NT):
                    m = nc.tensor.matmul((Y, X)[c][:, t * SEQ:(t + 1) * SEQ],
                                         qT[rows, j * SEQ + t * P:j * SEQ + (t + 1) * P],
                                         kT[rows, j * SEQ:(j + 1) * SEQ], start=True, stop=True)
                m.then_inc(S[f"map{c}_full"], 1)

            def turn_probs(u, j):
                p = probs[:, j % 2, :]
                pe.wait_ge(S["probs_ready"], u.head(j) + 1)
                if j > 0:
                    pe.wait_ge(S["o_taken"], u.head(j))
                for t in range(NT):
                    for k in range(1 if u.kind == "G" else NT):
                        w, at = (P, t * P) if u.kind == "G" else (SEQ, k * SEQ + t * P)
                        m = nc.tensor.transpose(X[:, at:at + P], p[:, t * w + k * P:t * w + (k + 1) * P], ident)
                m.then_inc(S["pt_full"], 1)

            def weigh(u, j):
                pe.wait_ge(S["pt_ready"], u.head(j) + 1)
                if j == 0:
                    pe.wait_ge(S["proj_ready"], PROJ0[u.layer] + 3 * u.body)
                col = 2 * HEAD + (j // UH) * HEAD if u.kind == "D" else j * HEAD
                for t in range(NT):
                    if u.kind == "G":
                        m = nc.tensor.matmul(X[:, t * P:(t + 1) * P], pT[:, t * P:(t + 1) * P],
                                             unit[:, 2, t, col:col + HEAD], start=True, stop=True)
                    else:
                        for k in range(NT):
                            m = nc.tensor.matmul(X[:, t * P:(t + 1) * P], pT[:, k * SEQ + t * P:k * SEQ + (t + 1) * P],
                                                 unit[:, 2, k, col:col + HEAD], start=(k == 0), stop=(k == NT - 1))
                m.then_inc(S["o_full"], 1)

            def attention(u, h):
                if u is None:
                    return
                if u.kind == "D":
                    if h in (2, 3, 4):
                        qk_fills(u, {2: (0, 1), 3: (2, 3), 4: (4,)}[h])
                elif h in (2, 4):
                    qk_fills(u, {2: (0, 1), 4: (2, 3)}[h])
                for j in u.stages(h, 4):
                    weigh(u, j)
                for j in u.stages(h, 0):
                    if u.kind == "B":
                        score_map(u, j, 0)
                    else:
                        score(u, j)
                if u.kind == "B":
                    for j in u.stages(h, 1):
                        score_map(u, j, 1)
                for j in u.stages(h, 3):
                    turn_probs(u, j)

            pe.wait_ge(S["consts_in"], 16)
            pe.wait_ge(S["x_in"], 16 * NT)
            for layer in range(2):
                turn_x(layer, 0)
                turn_x(layer, 1)
                for u, b, i in loops(pe, layer):
                    for h in range(2 * BODY):
                        s, half = divmod(h, 2)
                        blk, c = divmod(s, CHUNKS)
                        if u is None and h < 8:
                            if 1 <= h <= 6:
                                turn_x(layer, h + 1)
                            pe.wait_ge(S["turn_taken"], 16 * layer + h + 1)
                        attention(u, h)
                        if c == 0 and half == 0:
                            if u is not None:
                                pe.wait_ge(S["proj_ready"], PROJ0[layer] + 3 * (b + i) + blk - 2)
                            elif layer == 1:
                                pe.wait_ge(S["y_scaled"], (3, 4, 2)[blk])
                        half_chunk(CHUNK0[layer] + BODY * (b + i) + s, (CHUNK0[layer] + s) % SPLIT,
                                   half, acc[blk], c * CK)
                B = BODIES[layer]
                g0 = CHUNK0[layer] + BODY * B
                for s in range(CHUNKS + len(OUT_ORDER)):
                    n, c = (-1, s) if s < CHUNKS else OUT_ORDER[s - CHUNKS]
                    tiles = acc[0 if n < 0 else OUT_SET[n]]
                    for half in range(2):
                        if half == 1 and s in TURN_SLOTS:
                            k = TURN_SLOTS.index(s)
                            if k == 0:
                                pe.wait_ge(S["o_taken"], CREDIT + HEADS[layer])
                            turn_mix(layer, k, 0)
                            turn_mix(layer, k, 1)
                        if half == 0 and c == 0:
                            if n < 3:
                                pe.wait_ge(S["proj_ready"], PROJ0[layer] + 3 * B + n - 1)
                            else:
                                pe.wait_ge(S["y_scaled"], OUT_BLOCKS * layer + 1)
                        if half == 0 and s >= CHUNKS:
                            pe.wait_ge(S["turn_taken"], 16 * layer + 8 + 2 * (c + 1))
                        half_chunk(g0 + s, (g0 + s) % SPLIT, half, tiles, c * CK)

        @block.scalar
        def _(act):
            def split_hi(at, i=0):
                if at >= ALL_CHUNKS:
                    return
                act.wait_ge(landed[at % RAW], 16 * (at // RAW + 1) + (16 * BODY // RAW) * i)
                if at >= SPLIT:
                    act.wait_ge(S["chunk_used"], at + BODY * i - SPLIT + 1)
                nc.scalar.activation(w_hi[:, at % SPLIT, :], raw[:, at % RAW, :], ACT.Copy).then_inc(S["hi_ready"], 1)

            def take(chunks, blk, dst):
                act.wait_ge(S["chunk_used"], chunks)
                for t in range(NT):
                    m = nc.scalar.activation(dst[:, t, :], acc[blk][t][:, :], ACT.Copy, scale=pre_r[:, t:t + 1])
                m.then_inc(S["proj_ready"], 1)

            def exps(u, j):
                act.wait_ge(S["negm_ready"], u.plain(j) + 1)
                if j >= 2:
                    act.wait_ge(S["pt_full"], u.head(j) - 1)
                if j == 0:
                    act.wait_ge(S["unit_done"], CREDIT + u.index)
                    act.wait_ge(S["pt_full"], u.head(0))
                w = P if u.kind == "G" else SEQ
                for t in range(NT):
                    m = nc.scalar.activation(probs[:, j % 2, t * w:(t + 1) * w], scores[:, j % 2, t * w:(t + 1) * w],
                                             ACT.Exp, bias=negm[:, 2 * j + t:2 * j + t + 1],
                                             accum_out=usum[:, 2 * j + t:2 * j + t + 1])
                m.then_inc(S["probs_ready"], 1)
                if u.kind == "D":
                    nc.scalar.activation(sinke[:, 2 * j:2 * j + 2], negm[:, 2 * j:2 * j + 2], ACT.Exp,
                                         bias=sinkb[:, j:j + 1]).then_inc(S["sink_ready"], 1)

            def exps_map(u, j, c):
                act.wait_ge(S[f"map{c}_neg"], u.diff(j) + 1)
                act.wait_ge(S["probs_ready"], u.head(j))
                for t in range(NT):
                    m = nc.scalar.activation(scores[:, c, t * SEQ:(t + 1) * SEQ], bank[1 - c][:, t * SEQ:(t + 1) * SEQ],
                                             ACT.Exp, bias=bneg[:, c, t:t + 1], scale=SCALE_B,
                                             accum_out=bsum[:, c, t:t + 1])
                m.then_inc(S[f"map{c}_exp"], 1)

            def attention(u, h):
                if u is None:
                    return
                if u.kind == "B":
                    for j in u.stages(h, 4):
                        act.wait_ge(S["o_full"], u.head(j) + 1)
                        act.wait_ge(S["o_squared"], CREDIT + u.diff(j))
                        if j == 0:
                            act.wait_ge(S["unit_done"], CREDIT + u.index)
                        for t in range(NT):
                            m = nc.scalar.activation(sqo[:, t * P:(t + 1) * P], X[:, t * P:(t + 1) * P], ACT.Square,
                                                     accum_out=usum[:, 2 * j + t:2 * j + t + 1])
                        m.then_inc(S["o_squared"], 1)
                    for j in u.stages(h, 1):
                        exps_map(u, j, 0)
                        exps_map(u, j, 1)
                else:
                    for j in u.stages(h, 1):
                        exps(u, j)
                if u.kind == "G" and h == 2 * BODY - 1:
                    act.wait_ge(S["m_diff"], u.index - 5)
                    nc.scalar.activation(wexp[:, :, :], dexp[:, :, :], ACT.Exp).then_inc(S["m_exp"], 1)

            def turned(f, layer):
                act.wait_ge(S["turn_full"], f + 1)
                for n in range(2):
                    kt = 2 * (f % 8) + n
                    src, dst = bank[f % 2][:, n * SEQ:(n + 1) * SEQ], act_hi[:, kt, :]
                    if f % 16 < 8:
                        m = nc.scalar.activation(dst, src, ACT.Copy, scale=preg[:, layer, kt:kt + 1])
                    elif layer == 0:
                        m = nc.scalar.activation(dst.rearrange("p (c b a) -> p c b a", c=4, b=4),
                                                 src.rearrange("p (a b c) -> p c b a", b=4, c=4), ACT.Copy)
                    else:
                        m = nc.scalar.activation(dst, src, ACT.Copy)
                m.then_inc(S["turn_hi"], 1)

            def pre_squares(layer, t):
                if layer == 1 and t == 0:
                    act.wait_ge(S["gate_done"], CHUNKS)
                    act.wait_ge(S["x_new"], NT * OUT_BLOCKS)
                if t == 1:
                    act.wait_ge(S["pre_sq"], 2 * layer + 1)
                for n, junk in enumerate((scores_flat, probs_flat)):
                    m = nc.scalar.activation(junk, resid[:, t, n * 1024:(n + 1) * 1024], ACT.Square,
                                             accum_out=pre_ss[:, t, n:n + 1])
                m.then_inc(S["pre_sq"], 1)

            split_hi(0)
            split_hi(1)
            act.wait_ge(S["lam_s"], 1)
            nc.scalar.activation(lame[:, :], lams[:, :], ACT.Exp).then_inc(S["lam_e"], 1)
            for layer in range(2):
                turned(16 * layer, layer)
                turned(16 * layer + 1, layer)
                for u, b, i in loops(act, layer):
                    for s in range(BODY):
                        if s % CHUNKS == 0 and (u is not None or s > 0):
                            blk = (2, 0, 1)[s // CHUNKS]
                            if u is None and s == 4:
                                act.wait_ge(S["pre_rdy"], layer + 1)
                            if u is not None and s == 0:
                                act.wait_ge(S["o_full"], u.head(0))
                            if u is not None and s > 0:
                                act.wait_ge(S["qk_full"], 4 * u.index + s // 2)
                            take(CHUNK0[layer] + BODY * (b + i) + s, blk, unit[:, blk, :, :])
                        if u is None and 1 <= 2 * s <= 6:
                            turned(16 * layer + 2 * s + 1, layer)
                        attention(u, 2 * s)
                        split_hi(CHUNK0[layer] + BODY * b + s + 2, i)
                        if u is None and 1 <= 2 * s + 1 <= 6:
                            turned(16 * layer + 2 * s + 2, layer)
                        attention(u, 2 * s + 1)
                        if u is None and s in (1, 2):
                            pre_squares(layer, s - 1)
                        if u is None and s == 3:
                            act.wait_ge(S["pre_var"], layer + 1)
                            nc.scalar.activation(std[:, :], var[:, :], ACT.Sqrt).then_inc(S["pre_std"], 1)
                g0 = CHUNK0[layer] + BODY * BODIES[layer]
                for s in range(CHUNKS + len(OUT_ORDER) + 1):
                    if s == 0:
                        act.wait_ge(S["o_full"], CREDIT + HEADS[layer])
                        take(g0, 2, unit[:, 2, :, :])
                        if layer == 0:
                            act.wait_ge(S["rs_v"], 1)
                            nc.scalar.activation(bstd[:, :], row_sum[:, 16:32], ACT.Sqrt).then_inc(S["rs_s"], 1)
                    if s == CHUNKS:
                        take(g0 + CHUNKS, 0, unit_out)
                    if s in OUT_SLOTS:
                        n = OUT_SLOTS.index(s)
                        done = OUT_BLOCKS * layer + n
                        act.wait_ge(S["chunk_used"], g0 + s)
                        act.wait_ge(S["y_sq"], done)
                        for t in range(NT):
                            m = nc.scalar.activation(probs[:, t, :], acc[OUT_SET[n]][t][:, :], ACT.Square,
                                                     accum_out=y_ss[:, t, n:n + 1])
                        m.then_inc(S["y_sq"], 1)
                    if s in GATE_SLOTS:
                        c = GATE_SLOTS.index(s)
                        if c == 0:
                            act.wait_ge(S["unit_done"], CREDIT + UNITS[layer])
                        else:
                            act.wait_ge(S["gate_u"], CHUNKS * layer + c)
                        src = unit_out_flat if c == 3 else unit[:, c, :, :].rearrange("p t n -> p (t n)")
                        if c >= 2:
                            act.wait_ge(S["proj_ready"], PROJ0[layer] + 3 * BODIES[layer] + c - 2)
                        nc.scalar.activation(scores_flat, src, ACT.Tanh, scale=0.5).then_inc(S["tanh_done"], 1)
                    split_hi(g0 + s + 2) if s < CHUNKS + len(OUT_ORDER) else None
                    if s in TURN_SLOTS:
                        c = TURN_SLOTS.index(s)
                        turned(16 * layer + 8 + 2 * c, layer)
                        turned(16 * layer + 9 + 2 * c, layer)
                act.wait_ge(S["y_var"], layer + 1)
                nc.scalar.activation(std[:, :], var[:, :], ACT.Sqrt).then_inc(S["y_std"], 1)

        @block.vector
        def _(dve):
            def split_lo(at, i=0):
                if at >= ALL_CHUNKS:
                    return
                dve.wait_ge(S["hi_ready"], at + BODY * i + 1)
                nc.vector.tensor_tensor(w_lo[:, at % SPLIT, :], raw[:, at % RAW, :],
                                        w_hi[:, at % SPLIT, :].bitcast(F32), ALU.subtract).then_inc(S["lo_ready"], 1)

            def turned(f, layer):
                dve.wait_ge(S["turn_hi"], f + 1)
                for n in range(2):
                    kt = 2 * (f % 8) + n
                    src, hi, lo = bank[f % 2][:, n * SEQ:(n + 1) * SEQ], act_hi[:, kt, :].bitcast(F32), act_lo[:, kt, :]
                    if f % 16 < 8:
                        m = nc.vector.scalar_tensor_tensor(lo, src, preg[:, layer, kt:kt + 1], hi, ALU.mult, ALU.subtract)
                    elif layer == 0:
                        m = nc.vector.tensor_tensor(lo.rearrange("p (c b a) -> p c b a", c=4, b=4),
                                                    src.rearrange("p (a b c) -> p c b a", b=4, c=4),
                                                    hi.rearrange("p (c b a) -> p c b a", c=4, b=4), ALU.subtract)
                    else:
                        m = nc.vector.tensor_tensor(lo, src, hi, ALU.subtract)
                m.then_inc(S["turn_taken"], 1)

            def take_qk(u, f):
                dve.wait_ge(S["qk_full"], 4 * u.index + f + 1)
                if u.kind == "D":
                    dst = (qT[:, 0:NB], qT[:, NB:2 * NB], unit_out_flat[:, 0:NB], unit_out_flat[:, NB:2 * NB],
                           kT[:, 0:NB])[f]
                else:
                    dst = (qT, kT)[f // 2][:, (f % 2) * NB:(f % 2 + 1) * NB]
                nc.vector.tensor_copy(dst, bank[f % 2][:, :]).then_inc(S["qk_ready"], 1)

            def mask_and_max(u, j):
                w = P if u.kind == "G" else SEQ
                dve.wait_ge(S["s_full"], u.plain(j) + 1)
                if u.kind == "A" and j == 0:
                    dve.wait_ge(S["bias_rdy"], 1)
                dve.wait_ge(S["probs_ready"], u.head(j) - 1 if j else u.head(0))
                dst = scores[:, j % 2, 0:NT * w]
                if u.kind == "G":
                    for t in range(NT):
                        m = nc.vector.scalar_tensor_tensor(dst[:, t * P:(t + 1) * P], Y[:, t * P:(t + 1) * P], SCALE,
                                                           const(u.mask), ALU.mult, ALU.add)
                else:
                    if u.kind == "A":
                        add = bias_a[:, bass.ds((UH * u.step + j) * NT * SEQ, NT * SEQ)]
                    else:
                        add = const(u.mask)
                    m = nc.vector.scalar_tensor_tensor(dst, Y[:, :], SCALE, add, ALU.mult, ALU.add)
                m.then_inc(S["masked"], 1)
                two = slice(2 * j, 2 * j + 2)
                dve.wait_ge(S["masked"], u.plain(j) + 1)
                nc.vector.reduce_max(rmax[:, two], dst.rearrange("p (t n) -> p t n", t=NT), AX_X).then_inc(S["maxed"], 1)
                dve.wait_ge(S["maxed"], u.plain(j) + 1)
                if u.kind == "D":
                    nc.vector.tensor_scalar(negm[:, two], rmax[:, two], -1.0, negsink[:, j:j + 1], ALU.mult,
                                            ALU.min).then_inc(S["negm_ready"], 1)
                else:
                    nc.vector.tensor_scalar(negm[:, two], rmax[:, two], -1.0, None, ALU.mult).then_inc(S["negm_ready"], 1)

            def max_map(u, j, c):
                dve.wait_ge(S[f"map{c}_full"], u.diff(j) + 1)
                nc.vector.reduce_max(bmax[:, c, :], bank[1 - c][:, :].rearrange("p (t n) -> p t n", t=NT),
                                     AX_X).then_inc(S[f"map{c}_max"], 1)
                dve.wait_ge(S[f"map{c}_max"], u.diff(j) + 1)
                nc.vector.tensor_scalar(bneg[:, c, :], bmax[:, c, :], -SCALE_B, None, ALU.mult).then_inc(
                    S[f"map{c}_neg"], 1)

            def combine(u, j):
                n = u.diff(j)
                dve.wait_ge(S["map0_exp"], n + 1)
                dve.wait_ge(S["map1_exp"], n + 1)
                nc.vector.reciprocal(binv[:, :, :], bsum[:, :, :]).then_inc(S["b_inv"], 1)
                dve.wait_ge(S["b_inv"], n + 1)
                nc.vector.tensor_scalar(bw[:, :], binv[:, 1, :], neglam[:, 0:1], None, ALU.mult).then_inc(S["b_w"], 1)
                for t in range(NT):
                    sl = slice(t * SEQ, (t + 1) * SEQ)
                    m = nc.vector.tensor_scalar(scores[:, 0, sl], scores[:, 0, sl], binv[:, 0, t:t + 1], None, ALU.mult)
                m.then_inc(S["b_scaled"], 1)
                dve.wait_ge(S["b_w"], n + 1)
                dve.wait_ge(S["b_scaled"], n + 1)
                dve.wait_ge(S["pt_full"], u.head(j) - 1 if j else u.head(0))
                for t in range(NT):
                    sl = slice(t * SEQ, (t + 1) * SEQ)
                    m = nc.vector.scalar_tensor_tensor(probs[:, j % 2, sl], scores[:, 1, sl], bw[:, t:t + 1],
                                                       scores[:, 0, sl], ALU.mult, ALU.add)
                m.then_inc(S["probs_ready"], 1)

            def take_pT(u, j):
                dve.wait_ge(S["pt_full"], u.head(j) + 1)
                dve.wait_ge(S["o_full"], u.head(j))
                n = SEQ if u.kind == "G" else 2 * SEQ
                nc.vector.tensor_copy(pT[:, 0:n], X[:, 0:n]).then_inc(S["pt_ready"], 1)

            def take_out(u, j):
                dve.wait_ge(S["o_full"], u.head(j) + 1)
                src = X[:, 0:NT * HEAD].rearrange("p (t d) -> p t d", t=NT)
                if u.kind == "G":
                    dst = unit_out[:, :, j * HEAD:(j + 1) * HEAD]
                elif u.kind == "D":
                    dst = mix[:, :, 2 * NB + j * HEAD:2 * NB + (j + 1) * HEAD]
                elif u.kind == "W":
                    dst = mix[:, :, bass.ds(NB * u.step + j * HEAD, HEAD)]
                else:
                    dst = mix[:, :, bass.ds(NB * u.index + j * HEAD, HEAD)]
                if u.kind == "B":
                    dve.wait_ge(S["o_squared"], CREDIT + u.diff(j) + 1)
                    nc.vector.tensor_tensor(dst, src, subg[:, :, :], ALU.mult).then_inc(S["o_taken"], 1)
                else:
                    nc.vector.tensor_scalar(dst, src, 1.0, None, ALU.mult).then_inc(S["o_taken"], 1)

            def close(u):
                if u.kind in ("A", "B"):
                    nc.vector.tensor_scalar(row_sum[:, bass.ds(8 * u.index, 8)], usum[:, 0:8], 1.0, None, ALU.mult).then_inc(S["unit_done"], 1)
                elif u.kind == "W":
                    nc.vector.tensor_scalar(row_sum[:, bass.ds(8 * u.step, 8)], usum[:, 0:8], 1.0, None, ALU.mult)
                    nc.vector.tensor_scalar(cneg[:, bass.ds(u.step, 1), :], negm[:, 0:8].rearrange("p (a n) -> p a n", a=1),
                                            1.0, None, ALU.mult).then_inc(S["unit_done"], 1)
                elif u.kind == "D":
                    dve.wait_ge(S["sink_ready"], 8)
                    nc.vector.tensor_tensor(row_sum[:, 16:32], usum[:, :], sinke[:, :], ALU.add).then_inc(S["unit_done"], 1)
                else:
                    n = u.index - 6
                    old_neg = cneg[:, bass.ds(u.step, 1), :].rearrange("p a n -> p (a n)")
                    total = row_sum[:, bass.ds(8 * u.step, 8)]
                    nc.vector.tensor_tensor(newneg[:, :], old_neg, negm[:, 0:8], ALU.min).then_inc(S["m_new"], 1)
                    dve.wait_ge(S["m_new"], n + 1)
                    nc.vector.tensor_tensor(dexp[:, 0, :], newneg[:, :], old_neg, ALU.subtract)
                    nc.vector.tensor_tensor(dexp[:, 1, :], newneg[:, :], negm[:, 0:8], ALU.subtract).then_inc(S["m_diff"], 1)
                    dve.wait_ge(S["m_diff"], n + 1)
                    nc.vector.tensor_scalar(old_neg, newneg[:, :], 1.0, None, ALU.mult)
                    dve.wait_ge(S["m_exp"], n + 1)
                    nc.vector.tensor_tensor(wsum[:, :], usum[:, 0:8], wexp[:, 1, :], ALU.mult)
                    nc.vector.tensor_tensor(total, total, wexp[:, 0, :], ALU.mult).then_inc(S["m_wsum"], 1)
                    dve.wait_ge(S["o_taken"], u.head(UH))
                    for t in range(NT):
                        old = mix[:, t, bass.ds(NB * u.step, NB)].rearrange("p (h d) -> p h d", h=UH)
                        new = unit_out[:, t, :].rearrange("p (h d) -> p h d", h=UH)
                        w = [wexp[:, k, :].rearrange("p (h t) -> p t h", t=NT)[:, t, :].unsqueeze(2).to_broadcast([P, UH, HEAD])
                             for k in range(2)]
                        nc.vector.tensor_tensor(old, old, w[0], ALU.mult)
                        m = nc.vector.tensor_tensor(new, new, w[1], ALU.mult)
                    m.then_inc(S["m_scaled"], 1)
                    dve.wait_ge(S["m_wsum"], n + 1)
                    nc.vector.tensor_tensor(total, total, wsum[:, :], ALU.add)
                    dve.wait_ge(S["m_scaled"], n + 1)
                    for t in range(NT):
                        old = mix[:, t, bass.ds(NB * u.step, NB)]
                        m = nc.vector.tensor_tensor(old, old, unit_out[:, t, :], ALU.add)
                    m.then_inc(S["unit_done"], 1)

            def attention(u, h):
                if u is None:
                    return
                if u.kind == "D":
                    fills = {2: (0, 1), 3: (2, 3), 4: (4,)}.get(h, ())
                else:
                    fills = {2: (0, 1), 4: (2, 3)}.get(h, ())
                for f in fills:
                    take_qk(u, f)
                for j in u.stages(h, 4):
                    take_out(u, j)
                if u.kind == "B":
                    for j in u.stages(h, 0):
                        max_map(u, j, 0)
                    for j in u.stages(h, 1):
                        max_map(u, j, 1)
                    for j in u.stages(h, 2):
                        combine(u, j)
                else:
                    for j in u.stages(h, 0):
                        mask_and_max(u, j)
                for j in u.stages(h, 3):
                    take_pT(u, j)
                if h == 2 * BODY - 1:
                    close(u)

            def gate(layer, c):
                n = CHUNKS * layer + c
                src = unit_out_flat if c == 3 else unit[:, c, :, :].rearrange("p t n -> p (t n)")
                dve.wait_ge(S["tanh_done"], n + 1)
                if n:
                    dve.wait_ge(S["gate_done"], n)
                nc.vector.scalar_tensor_tensor(probs_flat, scores_flat, 1.0, src, ALU.add, ALU.mult).then_inc(S["gate_u"], 1)
                dve.wait_ge(S["gate_u"], n + 1)
                if c == 0:
                    dve.wait_ge(S["rs_rdy"], layer + 1)
                for t in range(NT):
                    for hh in range(UH):
                        o = mix[:, t, c * NB + hh * HEAD:c * NB + (hh + 1) * HEAD]
                        k = 8 * c + 2 * hh + t
                        m = nc.vector.scalar_tensor_tensor(o, o, row_scale[:, k:k + 1],
                                                           probs[:, t, hh * HEAD:(hh + 1) * HEAD], ALU.mult, ALU.mult)
                m.then_inc(S["gate_done"], 1)

            dve.wait_ge(S["vecs_in"], 80)
            lv = lamv[:, :, :].rearrange("p (a b) n -> p a b n", a=2)
            nc.vector.tensor_tensor(lamp[:, :, :], lv[:, :, 0, :], lv[:, :, 1, :], ALU.mult).then_inc(S["lam_p"], 1)
            dve.wait_ge(S["lam_p"], 1)
            nc.vector.reduce_sum(lams[:, :], lamp[:, :, :], AX_X).then_inc(S["lam_s"], 1)
            nc.vector.tensor_scalar(negsink[:, :], sinkb[:, :], -1.0, None, ALU.mult).then_inc(S["negsink_rdy"], 1)
            split_lo(0)
            split_lo(1)
            dve.wait_ge(S["lam_e"], 1)
            nc.vector.scalar_tensor_tensor(neglam[:, :], lame[:, 1:2], -LAMBDA_INIT, lame[:, 0:1], ALU.add,
                                           ALU.subtract).then_inc(S["lam_rdy"], 1)
            for layer in range(2):
                turned(16 * layer, layer)
                turned(16 * layer + 1, layer)
                for u, b, i in loops(dve, layer):
                    for s in range(BODY):
                        if u is None and 1 <= 2 * s <= 6:
                            turned(16 * layer + 2 * s + 1, layer)
                        attention(u, 2 * s)
                        if u is None and s == 3:
                            dve.wait_ge(S["pre_sq"], 2 * layer + 2)
                            nc.vector.reduce_sum(ss[:, :], pre_ss[:, :, 0:2], AX_X).then_inc(S["pre_sum"], 1)
                            dve.wait_ge(S["pre_sum"], layer + 1)
                            nc.vector.tensor_scalar(var[:, :], ss[:, :], 1.0 / D_MODEL, EPS, ALU.mult,
                                                    ALU.add).then_inc(S["pre_var"], 1)
                        split_lo(CHUNK0[layer] + BODY * b + s + 2, i)
                        if u is None and s == 3:
                            dve.wait_ge(S["pre_std"], layer + 1)
                            nc.vector.reciprocal(pre_r[:, :], std[:, :]).then_inc(S["pre_rdy"], 1)
                        if u is None and 1 <= 2 * s + 1 <= 6:
                            turned(16 * layer + 2 * s + 2, layer)
                        attention(u, 2 * s + 1)
                        if layer == 0 and u is None and s == 6:
                            dve.wait_ge(S["bias_in"], 16 * 32)
                            dve.wait_ge(S["consts_in"], 16)
                            for g in range(8 * NT):
                                turned_keys, keys = (v[:, g * SEQ:(g + 1) * SEQ].rearrange("p (j k) -> p j k", j=ROWS)
                                                     for v in (bias_in, bias_a))
                                mask = const("mask_a").rearrange("p (j k) -> p j k", j=ROWS)
                                m = nc.vector.tensor_tensor(keys, turned_keys[:, :, ::-1], mask, ALU.add)
                            m.then_inc(S["bias_rdy"], 1)
                g0 = CHUNK0[layer] + BODY * BODIES[layer]
                for s in range(CHUNKS + len(OUT_ORDER) + 1):
                    if s == 0:
                        dve.wait_ge(S["unit_done"], CREDIT + UNITS[layer])
                        n = 16 if layer == 0 else 32
                        m = nc.vector.tensor_scalar(row_sum[:, 0:n], row_sum[:, 0:n], 2.0, None, ALU.mult)
                        if layer == 0:
                            up = (0.5 * (1.0 - LAMBDA_INIT)) ** -2
                            m = nc.vector.tensor_scalar(row_sum[:, 16:32], row_sum[:, 16:32], up / HEAD, up * EPS,
                                                        ALU.mult, ALU.add)
                        m.then_inc(S["rs_v"], 1)
                        dve.wait_ge(S["rs_v"], layer + 1)
                        m = nc.vector.reciprocal(row_scale[:, 0:n], row_sum[:, 0:n])
                        if layer == 0:
                            dve.wait_ge(S["rs_s"], 1)
                            m = nc.vector.reciprocal(row_scale[:, 16:32], bstd[:, :])
                        m.then_inc(S["rs_rdy"], 1)
                    if s in OUT_SLOTS:
                        n = OUT_SLOTS.index(s)
                        if n == 0:
                            dve.wait_ge(S["postg_in"], 16 * (layer + 1))
                        dve.wait_ge(S["y_sq"], OUT_BLOCKS * layer + n + 1)
                        for t in range(NT):
                            m = nc.vector.tensor_tensor(mix[:, t, n * NB:(n + 1) * NB], acc[OUT_SET[n]][t][:, :],
                                                        postg[:, n * NB:(n + 1) * NB], ALU.mult)
                        m.then_inc(S["y_scaled"], 1)
                    if s in GATE_SLOTS:
                        gate(layer, GATE_SLOTS.index(s))
                    split_lo(g0 + s + 2) if s < CHUNKS + len(OUT_ORDER) else None
                    if s in TURN_SLOTS:
                        c = TURN_SLOTS.index(s)
                        turned(16 * layer + 8 + 2 * c, layer)
                        turned(16 * layer + 9 + 2 * c, layer)
                nc.vector.reduce_sum(ss[:, :], y_ss[:, :, :], AX_X).then_inc(S["y_sum"], 1)
                dve.wait_ge(S["y_sum"], layer + 1)
                nc.vector.tensor_scalar(var[:, :], ss[:, :], 1.0 / D_MODEL, EPS, ALU.mult, ALU.add).then_inc(S["y_var"], 1)
                dve.wait_ge(S["y_std"], layer + 1)
                nc.vector.reciprocal(post_r[:, :], std[:, :]).then_inc(S["y_rdy"], 1)
                dve.wait_ge(S["y_rdy"], layer + 1)
                dve.wait_ge(S["resid_in"], 16 * NT)
                for n in range(OUT_BLOCKS):
                    for t in range(NT):
                        cols = slice(n * NB, (n + 1) * NB)
                        nc.vector.scalar_tensor_tensor(resid[:, t, cols], mix[:, t, cols], post_r[:, t:t + 1],
                                                       resid[:, t, cols], ALU.mult, ALU.add).then_inc(S["x_new"], 1)


def constants():
    f = np.float32
    p = np.arange(P)
    made = {"ident": np.eye(P, dtype=f)}
    col, key = p % GRID_W, np.arange(SEQ) % GRID_W
    start = np.clip(col - 8, 0, GRID_W - 16)
    ok = (key[None] >= start[:, None]) & (key[None] < start[:, None] + 16)
    made["mask_a"] = np.where(ok, f(0), f(NEG))
    tok = token_order()

    def window(half):
        q = tok.reshape(NT, P).T
        ok = np.abs(q[:, :, None] - tok[None, None]) <= half
        return np.where(ok, f(0), f(NEG)).reshape(P, NT * SEQ)

    made["mask_w"], made["mask_d"] = window(64), window(128)
    for name, n in (("mask_g1", 64), ("mask_g2", 16)):
        made[name] = np.where(p[:, None] // n == p[None] // n, f(0), f(NEG))
    for layer, (half, groups, order) in enumerate(((8, 8, np.arange(SEQ)), (16, 4, tok))):
        inv = f(500000.0) ** (-np.arange(half, dtype=f) / f(half))
        ang = order.astype(f)[:, None] * inv.astype(f)[None]
        cos, sin = np.cos(ang).astype(f), np.sin(ang).astype(f)
        for name, tab in (("cos", [cos, cos]), ("sin", [-sin, sin])):
            tab = np.concatenate(tab, 1).reshape(NT, P, 1, 2 * half).transpose(1, 0, 2, 3)
            made[f"{name}{layer}"] = np.broadcast_to(tab, (P, NT, groups, 2 * half)).reshape(P, -1)
    return np.ascontiguousarray(np.concatenate([made[n].astype(f) for n in CONST_COLS], 1))


def token_order():
    return np.arange(SEQ).reshape(16, 4, 4).transpose(2, 1, 0).reshape(-1)


def in_blocks():
    a = [[base + 512 * u for base in (0, 1024, 2048)] for u in range(2)]
    b = [[base + 512 * u for base in (4096, 5120, 6144)] for u in range(2)]
    first = sum(a + b, []) + [3072, 3584, 7168, 7680]
    c = [[base + 1024 * g + 512 * u for base in (0, 3072, 6144)] for g in range(3) for u in range(2)]
    second = sum(c, []) + [10240, 10752, 11264] + [9216, 9728, 11776, 12288]
    return first, second


def pack_weights(w_ins, w_outs):
    packed = np.empty((ALL_CHUNKS, P, CK, NB), np.float32)
    g = 0
    for w_in, w_out, starts in zip(w_ins, w_outs, in_blocks()):
        places = [(w_in, s, c) for s in starts for c in range(CHUNKS)]
        places += [(w_out, n * NB, c) for n, c in OUT_ORDER]
        for w, s, c in places:
            packed[g] = w[c * CK * P:(c + 1) * CK * P, s:s + NB].reshape(CK, P, NB).transpose(1, 0, 2)
            g += 1
    return packed.reshape(ALL_CHUNKS, P, CK * NB)


def kernel(**inputs):
    import concourse.bacc as _bacc
    from concourse.bass_utils import run_bass_kernel_spmd as _run

    x = {k: np.asarray(v) for k, v in inputs.items()}
    order = token_order()
    rows = x["x"].reshape(SEQ, D_MODEL)
    per_k = lambda g: g.reshape(KT, P).T
    arrays = {
        "weights": pack_weights((x["l0_w_in"], x["l1_w_in"]), (x["l0_w_out"], x["l1_w_out"])),
        "x_nat": rows,
        "x_perm": rows[order],
        "consts": constants(),
        "pre_g": np.stack([per_k(x["l0_pre_g"]), per_k(x["l1_pre_g"])], 1),
        "post_g": np.stack([x["l0_post_g"], x["l1_post_g"]]),
        "rpb": x["l0_rpb"][:, :, ::-1].reshape(-1),
        "lam": np.concatenate([x["l0_lam_q1"], x["l0_lam_k1"], x["l0_lam_q2"], x["l0_lam_k2"]]),
        "subln": x["l0_subln_g"],
        "sink": x["l1_sink"],
    }
    arrays = {k: np.ascontiguousarray(v) for k, v in arrays.items()}
    nc = _bacc.Bacc("TRN2", target_bir_lowering=False, num_devices=1)
    args = [nc.dram_tensor(k, v.shape, mybir.dt.from_np(v.dtype), kind="ExternalInput").ap() for k, v in arrays.items()]
    out = nc.dram_tensor("out_0", (SEQ, D_MODEL), F32, kind="ExternalOutput").ap()
    build(nc, *args, out)
    r = _run(nc, [arrays], core_ids=[0])
    got = np.empty((SEQ, D_MODEL), np.float32)
    got[order] = r.results[0]["out_0"]
    return got.reshape(1, SEQ, D_MODEL)
```

```python
from contextlib import ExitStack

import numpy as np
import concourse.bass as bass
from concourse import mybir

ALU = mybir.AluOpType
ACT = mybir.ActivationFunctionType
AX_X = mybir.AxisListType.X
F32 = mybir.dt.float32
F32R = mybir.dt.float32r

P = 128
SEQ = 256
D_MODEL = 2048
NT = SEQ // P
KT = D_MODEL // P
NB = 512
CK = 4
CHUNKS = KT // CK
HEAD = 128
UH = NB // HEAD
BODY = 3 * CHUNKS
RAW = 4
SPLIT = 3
NEG = -1.0e30
EPS = 1e-6
OUT_BLOCKS = D_MODEL // NB
GRID_W = 64
ROWS = SEQ // GRID_W
RPB_R, RPB_C = 15, 31
SCALE = HEAD ** -0.5
SCALE_B = (HEAD // 2) ** -0.5
LAMBDA_INIT = 0.2

CREDIT = 1
CREDITED = ("o_full", "o_taken", "pt_full", "pt_ready", "probs_ready", "unit_done", "o_squared", "roped")

BODIES = (5, 8)
LAYER_CHUNKS = [n * BODY + CHUNKS + OUT_BLOCKS * CHUNKS for n in BODIES]
CHUNK0 = (0, LAYER_CHUNKS[0])
ALL_CHUNKS = sum(LAYER_CHUNKS)
OUT_ORDER = ([(0, c) for c in range(3)] + [(1, c) for c in range(3)] + [(0, 3), (1, 3)]
             + [(2, c) for c in range(4)] + [(3, c) for c in range(4)])
OUT_SET = (1, 2, 0, 1)
START = ((0, 0), (1, 0), (0, 1), (1, 1), (2, 0), (2, 1), (3, 0), (3, 1))
GATE_SLOTS = (0, 1, 3, 5)
TURN_SLOTS = (2, 4, 5, 7)
OUT_SLOTS = tuple(CHUNKS + OUT_ORDER.index((n, 3)) + 1 for n in range(OUT_BLOCKS - 1))
LAST = CHUNKS + len(OUT_ORDER) - 1
RS_WAITS = {(0, 0): 1, (0, 2): 2, (1, 0): 3}
HEADS = (16, 48)
UNITS = (4, 11)
PROJ0 = (0, 3 * BODIES[0] + 1)

PARTS = ((0, 0), (0, 1), (1, 0))

CONST_COLS = {}
_at = 0
for _name, _n in (("mask_a", SEQ), ("mask_w", NT * SEQ), ("mask_g1", P), ("mask_g2", P),
                  ("mask_d", NT * SEQ), ("cos0", NT * 16), ("sin0", NT * 16), ("cos1", NT * 32), ("sin1", NT * 32)):
    CONST_COLS[_name] = (_at, _n)
    _at += _n
CONST_N = _at


class Unit:

    def __init__(self, kind, layer, body, index, step=0, mask=None):
        self.kind, self.layer, self.mask = kind, layer, mask
        self.step = step
        self.body = body + step
        self.index = index + step
        self.heads = 8 if kind == "D" else UH

    def head(self, j):
        return CREDIT + UH * self.index + j

    def plain(self, j):
        return UH * self.index + j - (2 * UH if self.layer else 0)

    def diff(self, j):
        return UH * self.index + j - 2 * UH

    def at(self, j):
        return 5 + 2 * j if self.kind == "D" else 5 + 4 * j

    def fills(self, h):
        if self.kind == "D":
            return {2: (0, 1), 3: (2, 3), 4: (4,)}.get(h, ())
        return {2: (0, 1), 4: (2, 3)}.get(h, ())

    def stages(self, h, *offsets):
        return [j for j in range(self.heads) if h - self.at(j) in offsets]


ATTENTION = [
    ("A", 0, 1, 0, 2, None), ("B", 0, 3, 2, 2, None),
    ("W", 1, 1, 4, 2, "mask_w"), ("G", 1, 3, 6, 2, "mask_g1"), ("G", 1, 5, 8, 2, "mask_g2"),
    ("D", 1, 7, 10, 1, "mask_d"),
]


def build(nc, weights, x_turned, x_nat, x_perm, consts, identity, pre_g, post_g, rpb, lam, subln, sink, out):
    with ExitStack() as ctx:
        def sb(name, shape, dt=F32):
            return ctx.enter_context(nc.sbuf_tensor(name, shape, dt))

        def sem(name):
            return ctx.enter_context(nc.semaphore(name))

        credit = sb("credit", [P, len(CREDITED)])
        raw = sb("raw", [P, RAW, CK * NB])
        w_hi = sb("w_hi", [P, SPLIT, CK * NB], F32R)
        w_lo = sb("w_lo", [P, SPLIT, CK * NB], F32R)
        act_hi = sb("act_hi", [P, KT, SEQ], F32R)
        act_lo = sb("act_lo", [P, KT, SEQ], F32R)
        unit = sb("unit", [P, 3, NT, NB])
        mix = sb("mix", [P, NT, D_MODEL])
        resid = sb("resid", [P, NT, D_MODEL])
        qT = [sb(f"qT_{part}", [P, UH * SEQ], F32R) for part in ("hi", "lo")]
        kT = [sb(f"kT_{part}", [P, UH * SEQ], F32R) for part in ("hi", "lo")]
        scores = sb("scores", [P, 2, NT * SEQ])
        probs = sb("probs", [P, 2, NT * SEQ])
        late_k = sb("late_k", [P, SEQ])
        pT = sb("pT", [P, 2 * SEQ])
        unit_out = sb("unit_out", [P, NT, NB])
        ident = sb("ident", [P, P])
        cst = sb("cst", [P, CONST_N])
        postg = sb("postg", [P, D_MODEL])
        preg = sb("preg", [P, 2, KT])
        rope_c = sb("rope_c", [P, 256])
        rope_s = sb("rope_s", [P, 256])
        lamv = sb("lamv", [P, 4, 64])
        lamp = sb("lamp", [P, 2, 64])
        lams = sb("lams", [P, 2])
        lame = sb("lame", [P, 2])
        neglam = sb("neglam", [P, 1])
        subg = sb("subg", [P, HEAD])
        sinkb = sb("sinkb", [P, 8])
        negsink = sb("negsink", [P, 8])
        pre_ss = sb("pre_ss", [P, NT, 4])
        y_ss = sb("y_ss", [P, NT, OUT_BLOCKS])
        ss = sb("ss", [P, NT])
        var = sb("var", [P, NT])
        warm = sb("warm", [P, 1])
        std = sb("std", [P, NT])
        pre_r = sb("pre_r", [P, NT])
        post_r = sb("post_r", [P, NT])
        rmax = sb("rmax", [P, 16])
        negm = sb("negm", [P, 16])
        usum = sb("usum", [P, 16])
        sinke = sb("sinke", [P, 16])
        bmax = sb("bmax", [P, 2, NT])
        bneg = sb("bneg", [P, 2, NT])
        bsum = sb("bsum", [P, 2, NT])
        binv = sb("binv", [P, 2, NT])
        bw = sb("bw", [P, NT])
        cneg = sb("cneg", [P, 2, 8])
        newneg = sb("newneg", [P, 8])
        dexp = sb("dexp", [P, 2, 8])
        wexp = sb("wexp", [P, 2, 8])
        wsum = sb("wsum", [P, 8])
        row_sum = sb("row_sum", [P, 32])
        row_scale = sb("row_scale", [P, 32])
        bstd = sb("bstd", [P, 16])
        xT = resid[:, :, :].rearrange("p t (k n) -> p (t k) n", n=SEQ)
        x_halves = [[postg[:, 0:1024], postg[:, 1024:]],
                    [v[:, :, :].rearrange("p a n -> p (a n)") for v in (scores, probs)]]
        bias_in = mix[:, :, :].rearrange("p t n -> p (t n)")
        bias_a = resid[:, :, :].rearrange("p t n -> p (t n)")
        scores_flat = scores[:, :, :].rearrange("p a n -> p (a n)")
        probs_flat = probs[:, :, :].rearrange("p a n -> p (a n)")
        unit_out_flat = unit_out[:, :, :].rearrange("p t n -> p (t n)")
        g_qT, g_kT = postg[:, 0:UH * SEQ], postg[:, UH * SEQ:]

        acc = [[ctx.enter_context(nc.psum_tensor(f"acc{s}_{t}", [P, NB], F32)) for t in range(NT)]
               for s in range(3)]
        bank = [ctx.enter_context(nc.psum_tensor(f"bank_{n}", [P, NB], F32)) for n in ("x", "y")]
        X, Y = bank

        names = ("ident_in consts_in preg_in vecs_in resid_in postg_in out_sent "
                 "nat_in first_in first_hi first_lo hi_ready lo_ready chunk_used tile_done proj_ready roped rope_a "
                 "turn_full turn_hi turn_taken qk_full qk_hi qk_ready "
                 "s_full masked maxed negm_ready probs_ready sink_ready "
                 "map0_full map1_full map0_max map1_max map0_neg map1_neg map0_exp map1_exp b_inv b_w b_scaled "
                 "pt_full pt_ready o_full o_squared o_taken unit_done "
                 "m_new m_diff m_exp m_wsum m_scaled "
                 "pre_sq pre_sum pre_var pre_std pre_rdy lam_p lam_s lam_e bias_rdy "
                 "y_sq y_scaled y_sum y_var y_std y_rdy "
                 "rs_v rs_s rs_rdy tanh_done gate_u gate_done").split()
        S = {n: sem(n) for n in names}
        x_in = [sem(f"x_in{h}") for h in range(2 * CHUNKS)]
        x_new = [sem(f"x_new{t}") for t in range(NT)]
        landed = [sem(f"landed{i}") for i in range(RAW)]
        bias_in_two = [sem(f"bias_in_two{i}") for i in range(UH)]

        def const(name):
            a, n = CONST_COLS[name]
            return cst[:, a:a + n]

        def loops(eng, layer):
            yield None, 0, 0
            for kind, lay, body, index, count, mask in ATTENTION:
                if lay != layer:
                    continue
                if count == 1:
                    yield Unit(kind, lay, body, index, 0, mask), body, 0
                else:
                    with eng.Fori(0, count) as i:
                        yield Unit(kind, lay, body, index, i, mask), body, i

        def qk_parts(u, f):
            if u.kind == "G" or u.kind == "D" and f in (2, 3):
                return None
            if u.kind == "D" and f == 4:
                return kT[0][:, 0:SEQ], kT[1][:, 0:SEQ], SEQ
            return *(v[:, f % 2 * NB:(f % 2 + 1) * NB] for v in (qT, kT)[f // 2]), NB

        block = ctx.enter_context(nc.Block())

        @block.sync
        def _(sp):
            def load_x(h):
                sp.dma_start(xT[:, 2 * h:2 * h + 2, :], x_turned[:, 2 * h:2 * h + 2, :]).then_inc(x_in[h], 16)

            for half in range(2):
                load_x(half)
                cols = slice(half * CK * NB // 2, (half + 1) * CK * NB // 2)
                sp.dma_start(raw[:, 0, cols], weights[0][:, cols]).then_inc((S["first_in"], landed[0])[half], 16)
            for c in range(1, RAW):
                sp.dma_start(raw[:, c, :], weights[c]).then_inc(landed[c], 16)
                load_x(2 * c)
                load_x(2 * c + 1)
            with sp.Fori(1, ALL_CHUNKS // RAW) as n:
                src = [sp.snap(n * RAW + r) for r in range(RAW)]
                free = [sp.snap(n * RAW + r - RAW + 1) for r in range(RAW)]
                for r in range(RAW):
                    sp.wait_ge(S["lo_ready"], free[r])
                    sp.dma_start(raw[:, r, :], weights[bass.ds(src[r], 1)].rearrange("a p n -> p (a n)")).then_inc(
                        landed[r], 16)
            for t in range(NT):
                for n in range(OUT_BLOCKS):
                    cols = slice(n * NB, (n + 1) * NB)
                    sp.wait_ge(x_new[t], OUT_BLOCKS + n + 1)
                    sp.dma_start(out[t * P:(t + 1) * P, cols], resid[:, t, cols]).then_inc(S["out_sent"], 16)
            sp.wait_ge(S["out_sent"], 16 * NT * OUT_BLOCKS)

        @block.gpsimd
        def _(pool):
            for n, name in enumerate(CREDITED):
                pool.memset(credit[:, n:n + 1], 0.0).then_inc(S[name], CREDIT)
            pool.wait_ge(x_in[-1], 16)
            pool.dma_start(cst[:, :], consts).then_inc(S["consts_in"], 16)
            pool.dma_start(lamv[:, :, :].rearrange("p a b -> p (a b)"), lam.partition_broadcast(P)).then_inc(
                S["vecs_in"], 16)
            pool.dma_start(subg[:, :], subln.partition_broadcast(P)).then_inc(S["vecs_in"], 16)
            pool.dma_start(sinkb[:, :], sink.partition_broadcast(P)).then_inc(S["vecs_in"], 16)
            for h in range(8):
                for t in range(NT):
                    for half in range(2):
                        r = 2 * t + half
                        src = bass.AP(rpb.tensor, h * RPB_R * RPB_C + (7 - r) * RPB_C + 15 - (GRID_W - 1),
                                      [[1, GRID_W], [RPB_C, ROWS], [1, GRID_W]])
                        at = (h * NT + t) * SEQ
                        pool.dma_start(bias_in[half * 64:half * 64 + 64, at:at + SEQ].rearrange(
                            "p (j k) -> p j k", j=ROWS), src).then_inc(bias_in_two[h // 2], 16)
            pool.wait_ge(S["pre_sq"], NT)
            pool.dma_start(postg[:, :], post_g[0].partition_broadcast(P)).then_inc(S["postg_in"], 16)

            def rotate(u, k, blk, cols, group):
                width = group // 4
                groups = cols // group
                shape = [P, NT, groups, width]
                v = unit[:, blk, :, 0:cols].rearrange("p t (g c) -> p t g c", c=group)
                cos, sin = (const(f"{name}{u.layer}").rearrange("p (t c) -> p t c", t=NT).unsqueeze(2)
                            for name in ("cos", "sin"))
                rc, rs = (a[:, 0:NT * groups * width].rearrange("p (t g c) -> p t g c", t=NT, c=width)
                          for a in (rope_c, rope_s))
                h = width // 2
                idx = (slice(None),) * 3
                first, second, whole = idx + (slice(0, h),), idx + (slice(h, width),), idx + (slice(0, width),)
                count = 2 * (u.index - 2) + k
                pool.tensor_tensor(rc, v[whole], cos.to_broadcast(shape), ALU.mult).then_inc(S["rope_a"], 1)
                pool.tensor_tensor(rs[first], v[second], sin[first].to_broadcast(shape[:3] + [h]),
                                   ALU.mult).then_inc(S["rope_a"], 1)
                pool.tensor_tensor(rs[second], v[first], sin[second].to_broadcast(shape[:3] + [h]),
                                   ALU.mult).then_inc(S["rope_a"], 1)
                pool.wait_ge(S["rope_a"], 3 * count + 3)
                pool.tensor_tensor(v[whole], rc, rs, ALU.add).then_inc(S["roped"], 1)

            pool.wait_ge(S["consts_in"], 16)
            for layer in range(2):
                for u, _, _ in loops(pool, layer):
                    if u is None or u.kind == "A":
                        continue
                    turns = ((0, NB), (1, NB), (2, 2 * HEAD)) if u.kind == "D" else ((0, NB), (1, NB))
                    for k, (blk, cols) in enumerate(turns):
                        pool.wait_ge(S["proj_ready"], PROJ0[layer] + 3 * u.body - 2 + k)
                        pool.wait_ge(S["roped"], CREDIT + 2 * (u.index - 2) + k)
                        rotate(u, k, blk, cols, HEAD // 2 if layer == 0 else HEAD)
                if layer == 0:
                    pool.wait_ge(S["masked"], 2 * UH)
                    for t in range(NT):
                        pool.dma_start(resid[:, t, :], x_perm[t * P:(t + 1) * P, :]).then_inc(S["resid_in"], 16)
            pool.wait_ge(S["masked"], UH * 8)
            pool.dma_start(postg[:, :], post_g[1].partition_broadcast(P)).then_inc(S["postg_in"], 16)

        @block.tensor
        def _(pe):
            def products(g, buf, places, tiles, first, done=None, lower=None):
                if places[0] == (0, 0):
                    pe.wait_ge(S["lo_ready"], g + 1)
                terms = [(kk, t, act_hi, w) for kk, t in places for w in (w_hi, w_lo)]
                terms += [(kk, t, act_lo, w_hi) for kk, t in places]
                for n, (kk, t, a, w) in enumerate(terms):
                    if lower is not None and n == 2 * len(places):
                        pe.wait_ge(S["turn_taken"], lower)
                    kt = first + kk
                    m = nc.tensor.matmul(tiles[t][:, :], a[:, kt, t * P:(t + 1) * P], w[:, buf, kk * NB:(kk + 1) * NB],
                                         start=(kt == 0 and a is act_hi and w is w_hi),
                                         stop=(kt == KT - 1 and a is act_lo))
                if done is not None:
                    m.then_inc(done, 1)

            def half_chunk(g, buf, half, tiles, first, lower=None):
                products(g, buf, [(kk, t) for kk in (2 * half, 2 * half + 1) for t in range(NT)], tiles, first,
                         S["chunk_used"] if half == 1 else None, lower)

            def tile_chunk(g, buf, t, tiles, first, lower=None, first_done=None):
                products(g, buf, [(kk, t) for kk in range(CK)], tiles, first,
                         S["chunk_used"] if t == 1 else first_done, lower)

            def first_products(half):
                for a, w, sem_ready, count in ((act_hi, w_hi, ("first_hi", "hi_ready")[half], 1),
                                               (act_hi, w_lo, ("first_lo", "lo_ready")[half], 1),
                                               (act_lo, w_hi, "turn_taken", half + 1)):
                    pe.wait_ge(S[sem_ready], count)
                    for kt in (2 * half, 2 * half + 1):
                        for t in range(NT):
                            m = nc.tensor.matmul(acc[0][t][:, :], a[:, kt, t * P:(t + 1) * P],
                                                 w[:, 0, kt * NB:(kt + 1) * NB],
                                                 start=(kt == 0 and a is act_hi and w is w_hi), stop=False)
                if half == 1:
                    m.then_inc(S["chunk_used"], 1)

            def turn(f, srcs):
                if f >= 2:
                    pe.wait_ge(S["turn_taken"], f - 1)
                for n, src in enumerate(srcs):
                    m = nc.tensor.transpose(bank[f % 2][:, n * P:(n + 1) * P], src, ident[:, :])
                m.then_inc(S["turn_full"], 1)

            def turn_x(k):
                c, t = START[k]
                pe.wait_ge(x_new[t], c + 1)
                turn(16 + k, [resid[:, t, kt * P:(kt + 1) * P] for kt in range(c * CK, (c + 1) * CK)])

            def turn_mix(layer, c, f):
                if f == 0:
                    pe.wait_ge(S["gate_done"], 4 * layer + c + 1)
                k = 2 * c + f
                turn(16 * layer + 8 + k,
                     [mix[:, t, kt * P:(kt + 1) * P] for kt in (2 * k, 2 * k + 1) for t in range(NT)])

            def qk_fills(u, fills):
                for f in fills:
                    if u.kind == "D":
                        blk, h0 = ((0, 0), (0, 2), (1, 0), (1, 2), (2, 0))[f]
                        need = (1, 1, 2, 2, 3)[f]
                    else:
                        blk, h0 = ((0, 0), (0, 2), (1, 0), (1, 2))[f]
                        need = (1, 1, 2, 2)[f]
                    if f == 0 and u.kind == "A":
                        pe.wait_ge(S["ident_in"], 16)
                    if f == 0:
                        pe.wait_ge(S["turn_taken"], 16 * u.layer + 8)
                        pe.wait_ge(S["o_taken"], u.head(0))
                    if f >= 2:
                        pe.wait_ge(S["qk_ready"], 4 * u.index + f - 1)
                    if u.kind == "A":
                        pe.wait_ge(S["proj_ready"], PROJ0[0] + 3 * (u.body - 1) + need)
                    else:
                        pe.wait_ge(S["roped"], CREDIT + 2 * (u.index - 2) + need)
                    for n, (h, t) in enumerate(((h0, 0), (h0, 1), (h0 + 1, 0), (h0 + 1, 1))):
                        m = nc.tensor.transpose(bank[f % 2][:, n * P:(n + 1) * P],
                                                unit[:, blk, t, h * HEAD:(h + 1) * HEAD], ident[:, :])
                    m.then_inc(S["qk_full"], 1)

            def score(u, j):
                jk = j // UH if u.kind == "D" else j
                pe.wait_ge(S["qk_ready"], 4 * u.index + (5 if u.kind == "D" else 4))
                if j > 0:
                    pe.wait_ge(S["masked"], u.plain(j))
                for t in range(NT):
                    keys, cols = ((slice(jk * SEQ + t * P, jk * SEQ + (t + 1) * P), slice(t * P, (t + 1) * P))
                                  if u.kind == "G" else
                                  (slice(jk * SEQ, (jk + 1) * SEQ), slice(t * SEQ, (t + 1) * SEQ)))
                    mine = slice(j % UH * SEQ + t * P, j % UH * SEQ + (t + 1) * P)
                    if u.kind == "G":
                        m = nc.tensor.matmul(Y[:, cols], g_qT[:, mine], g_kT[:, keys], start=True, stop=True)
                        continue
                    if j >= UH:
                        m = nc.tensor.matmul(Y[:, cols], unit_out_flat[:, mine], late_k[:, :], start=True, stop=True)
                        continue
                    for n, (a, b) in enumerate(PARTS):
                        m = nc.tensor.matmul(Y[:, cols], qT[a][:, mine], kT[b][:, keys],
                                             start=(n == 0), stop=(n == len(PARTS) - 1))
                m.then_inc(S["s_full"], 1)

            def score_map(u, j, c):
                if c == 0:
                    pe.wait_ge(S["qk_ready"], 4 * u.index + 4)
                    if j > 0:
                        pe.wait_ge(S["map0_exp"], u.diff(j))
                else:
                    if j > 0:
                        pe.wait_ge(S["o_taken"], u.head(j))
                rows = slice(64 * c, 64 * c + 64)
                for t in range(NT):
                    for n, (a, b) in enumerate(PARTS):
                        m = nc.tensor.matmul((Y, X)[c][:, t * SEQ:(t + 1) * SEQ],
                                             qT[a][rows, j * SEQ + t * P:j * SEQ + (t + 1) * P],
                                             kT[b][rows, j * SEQ:(j + 1) * SEQ], start=(n == 0), stop=(n == len(PARTS) - 1))
                m.then_inc(S[f"map{c}_full"], 1)

            def turn_probs(u, j):
                p = probs[:, j % 2, :]
                pe.wait_ge(S["probs_ready"], u.head(j) + 1)
                if j > 0:
                    pe.wait_ge(S["o_taken"], u.head(j))
                for t in range(NT):
                    for k in range(1 if u.kind == "G" else NT):
                        w, at = (P, t * P) if u.kind == "G" else (SEQ, k * SEQ + t * P)
                        m = nc.tensor.transpose(X[:, at:at + P], p[:, t * w + k * P:t * w + (k + 1) * P], ident[:, :])
                m.then_inc(S["pt_full"], 1)

            def weigh(u, j):
                pe.wait_ge(S["pt_ready"], u.head(j) + 1)
                if j == 0:
                    pe.wait_ge(S["proj_ready"], PROJ0[u.layer] + 3 * u.body)
                col = 2 * HEAD + (j // UH) * HEAD if u.kind == "D" else j * HEAD
                for t in range(NT):
                    if u.kind == "G":
                        m = nc.tensor.matmul(X[:, t * P:(t + 1) * P], pT[:, t * P:(t + 1) * P],
                                             unit[:, 2, t, col:col + HEAD], start=True, stop=True)
                    else:
                        for k in range(NT):
                            m = nc.tensor.matmul(X[:, t * P:(t + 1) * P], pT[:, k * SEQ + t * P:k * SEQ + (t + 1) * P],
                                                 unit[:, 2, k, col:col + HEAD], start=(k == 0), stop=(k == NT - 1))
                m.then_inc(S["o_full"], 1)

            def attention(u, h):
                if u is None:
                    return
                qk_fills(u, u.fills(h))
                for j in u.stages(h, 4):
                    weigh(u, j)
                for j in u.stages(h, 0):
                    if u.kind == "B":
                        score_map(u, j, 0)
                    else:
                        score(u, j)
                if u.kind == "B":
                    for j in u.stages(h, 1):
                        score_map(u, j, 1)
                for j in u.stages(h, 3):
                    turn_probs(u, j)

            for layer in range(2):
                if layer == 1:
                    turn_x(1)
                for u, b, i in loops(pe, layer):
                    for h in range(2 * BODY):
                        s, half = divmod(h, 2)
                        blk, c = divmod(s, CHUNKS)
                        if u is None and h < 8:
                            if layer == 1 and 1 <= h <= 6:
                                turn_x(h + 1)
                            pe.wait_ge(S["turn_hi"], 16 * layer + h + 1)
                        attention(u, h)
                        if c == 0 and half == 0:
                            if u is not None:
                                pe.wait_ge(S["proj_ready"], PROJ0[layer] + 3 * (b + i) + blk - 2)
                            elif layer == 1:
                                pe.wait_ge(S["y_scaled"], (3, 4, 2)[blk])
                        if layer == 0 and u is None and s == 0:
                            first_products(half)
                        elif layer == 0 and u is None and s < CHUNKS:
                            half_chunk(s, s % SPLIT, half, acc[0], c * CK, lower=h + 1)
                        elif u is None and s < CHUNKS:
                            c, t = START[h]
                            tile_chunk(CHUNK0[1] + c, (CHUNK0[1] + c) % SPLIT, t, acc[0], c * CK, lower=16 + h + 1)
                        else:
                            half_chunk(CHUNK0[layer] + BODY * (b + i) + s, (CHUNK0[layer] + s) % SPLIT, half,
                                       acc[blk], c * CK)
                B = BODIES[layer]
                g0 = CHUNK0[layer] + BODY * B
                for s in range(CHUNKS + len(OUT_ORDER) - 2):
                    n, c = (-1, s) if s < CHUNKS else OUT_ORDER[s - CHUNKS]
                    tiles = acc[0 if n < 0 else OUT_SET[n]]
                    for half in range(2):
                        if half == 0 and s in TURN_SLOTS:
                            k = TURN_SLOTS.index(s)
                            if k == 0:
                                pe.wait_ge(S["o_taken"], CREDIT + HEADS[layer])
                            turn_mix(layer, k, 0)
                            turn_mix(layer, k, 1)
                        if half == 0 and c == 0:
                            if n < 3:
                                pe.wait_ge(S["proj_ready"], PROJ0[layer] + 3 * B + n - 1)
                            else:
                                pe.wait_ge(S["y_scaled"], OUT_BLOCKS * layer + 1)
                        if half == 0 and s >= CHUNKS:
                            pe.wait_ge(S["turn_taken"], 16 * layer + 8 + 2 * (c + 1))
                        half_chunk(g0 + s, (g0 + s) % SPLIT, half, tiles, c * CK)
                for t in range(NT):
                    for s in range(CHUNKS + len(OUT_ORDER) - 2, CHUNKS + len(OUT_ORDER)):
                        n, c = OUT_ORDER[s - CHUNKS]
                        if layer == 0 and (t, c) == (1, CHUNKS - 1):
                            turn_x(0)
                        tile_chunk(g0 + s, (g0 + s) % SPLIT, t, acc[OUT_SET[n]], c * CK,
                                   first_done=S["tile_done"] if c == CHUNKS - 1 else None)

        @block.scalar
        def _(act):
            def split_hi(at, i=0):
                if at >= ALL_CHUNKS:
                    return
                if at == 0:
                    act.wait_ge(S["first_in"], 16)
                    nc.scalar.activation(w_hi[:, 0, 0:CK * NB // 2], raw[:, 0, 0:CK * NB // 2], ACT.Copy).then_inc(
                        S["first_hi"], 1)
                    act.wait_ge(landed[0], 16)
                    nc.scalar.activation(w_hi[:, 0, CK * NB // 2:], raw[:, 0, CK * NB // 2:], ACT.Copy).then_inc(
                        S["hi_ready"], 1)
                    return
                act.wait_ge(landed[at % RAW], 16 * (at // RAW + 1) + (16 * BODY // RAW) * i)
                if at >= SPLIT:
                    act.wait_ge(S["chunk_used"], at + BODY * i - SPLIT + 1)
                nc.scalar.activation(w_hi[:, at % SPLIT, :], raw[:, at % RAW, :], ACT.Copy).then_inc(S["hi_ready"], 1)

            def take(chunks, blk, dst):
                act.wait_ge(S["chunk_used"], chunks)
                for t in range(NT):
                    m = nc.scalar.activation(dst[:, t, :], acc[blk][t][:, :], ACT.Copy, scale=pre_r[:, t:t + 1])
                m.then_inc(S["proj_ready"], 1)

            def exps(u, j):
                act.wait_ge(S["negm_ready"], u.plain(j) + 1)
                if j >= 2:
                    act.wait_ge(S["pt_full"], u.head(j) - 1)
                if j == 0:
                    act.wait_ge(S["unit_done"], CREDIT + u.index)
                    act.wait_ge(S["pt_full"], u.head(0))
                w = P if u.kind == "G" else SEQ
                for t in range(NT):
                    m = nc.scalar.activation(probs[:, j % 2, t * w:(t + 1) * w], scores[:, j % 2, t * w:(t + 1) * w],
                                             ACT.Exp, bias=negm[:, 2 * j + t:2 * j + t + 1],
                                             accum_out=usum[:, 2 * j + t:2 * j + t + 1])
                m.then_inc(S["probs_ready"], 1)
                if u.kind == "D":
                    nc.scalar.activation(sinke[:, 2 * j:2 * j + 2], negm[:, 2 * j:2 * j + 2], ACT.Exp,
                                         bias=sinkb[:, j:j + 1]).then_inc(S["sink_ready"], 1)

            def exps_map(u, j, c):
                act.wait_ge(S[f"map{c}_neg"], u.diff(j) + 1)
                act.wait_ge(S["probs_ready"], u.head(j))
                for t in range(NT):
                    m = nc.scalar.activation(scores[:, c, t * SEQ:(t + 1) * SEQ], bank[1 - c][:, t * SEQ:(t + 1) * SEQ],
                                             ACT.Exp, bias=bneg[:, c, t:t + 1], scale=SCALE_B,
                                             accum_out=bsum[:, c, t:t + 1])
                m.then_inc(S[f"map{c}_exp"], 1)

            def take_qk(u, f):
                parts = qk_parts(u, f)
                if parts is None:
                    return
                act.wait_ge(S["qk_full"], 4 * u.index + f + 1)
                hi, _, n = parts
                nc.scalar.activation(hi, bank[f % 2][:, 0:n], ACT.Copy).then_inc(S["qk_hi"], 1)

            def attention(u, h):
                if u is None:
                    return
                for f in u.fills(h):
                    take_qk(u, f)
                if u.kind == "B":
                    for j in u.stages(h, 4):
                        act.wait_ge(S["o_full"], u.head(j) + 1)
                        act.wait_ge(S["o_squared"], CREDIT + u.diff(j))
                        if j == 0:
                            act.wait_ge(S["unit_done"], CREDIT + u.index)
                        for t in range(NT):
                            m = nc.scalar.activation(X[:, (NT + t) * P:(NT + t + 1) * P], X[:, t * P:(t + 1) * P], ACT.Square,
                                                     accum_out=usum[:, 2 * j + t:2 * j + t + 1])
                        m.then_inc(S["o_squared"], 1)
                    for j in u.stages(h, 1):
                        exps_map(u, j, 0)
                        exps_map(u, j, 1)
                else:
                    for j in u.stages(h, 1):
                        exps(u, j)
                if u.kind == "G" and h == 2 * BODY - 1:
                    act.wait_ge(S["m_diff"], u.index - 5)
                    nc.scalar.activation(wexp[:, :, :], dexp[:, :, :], ACT.Exp).then_inc(S["m_exp"], 1)

            def turned(f, layer):
                if f < 8:
                    act.wait_ge(x_in[f], 16)
                    for kt in (2 * f, 2 * f + 1):
                        m = nc.scalar.activation(act_hi[:, kt, :], xT[:, kt, :], ACT.Copy, scale=preg[:, 0, kt:kt + 1])
                    m.then_inc(S["turn_hi"], 1)
                    return
                act.wait_ge(S["turn_full"], f + 1 - 8)
                if 16 <= f < 24:
                    c, t = START[f - 16]
                    for kk in range(CK):
                        kt = c * CK + kk
                        m = nc.scalar.activation(act_hi[:, kt, t * P:(t + 1) * P], bank[f % 2][:, kk * P:(kk + 1) * P],
                                                 ACT.Copy, scale=preg[:, 1, kt:kt + 1])
                    m.then_inc(S["turn_hi"], 1)
                    return
                for n in range(2):
                    kt = 2 * (f % 8) + n
                    src, dst = bank[f % 2][:, n * SEQ:(n + 1) * SEQ], act_hi[:, kt, :]
                    if layer == 0:
                        m = nc.scalar.activation(dst.rearrange("p (c b a) -> p c b a", c=4, b=4),
                                                 src.rearrange("p (a b c) -> p c b a", b=4, c=4), ACT.Copy)
                    else:
                        m = nc.scalar.activation(dst, src, ACT.Copy)
                m.then_inc(S["turn_hi"], 1)

            def pre_squares(layer, t):
                if layer == 1 and t == 0:
                    act.wait_ge(S["gate_done"], CHUNKS)
                    for tile in range(NT):
                        act.wait_ge(x_new[tile], OUT_BLOCKS)
                if t == 1:
                    act.wait_ge(S["pre_sq"], 2 * layer + 1)
                if layer == 0 and t == 0:
                    act.wait_ge(S["nat_in"], 16 * 2 * NT)
                for n, junk in enumerate((unit_out_flat, unit[:, 2, :, :].rearrange("p t n -> p (t n)"))):
                    src = x_halves[t][n] if layer == 0 else resid[:, t, n * 1024:(n + 1) * 1024]
                    m = nc.scalar.activation(junk, src, ACT.Square,
                                             accum_out=pre_ss[:, t, n:n + 1])
                m.then_inc(S["pre_sq"], 1)

            act.dma_start(preg[:, :, :], pre_g).then_inc(S["preg_in"], 16)
            act.dma_start(ident[:, :], identity).then_inc(S["ident_in"], 16)
            act.wait_ge(S["o_full"], CREDIT)
            nc.scalar.activation(warm[:, :], credit[:, 0:1], ACT.Copy)
            act.wait_ge(S["preg_in"], 16)
            turned(0, 0)
            for layer in range(2):
                if layer == 0:
                    split_hi(0)
                turned(16 * layer + 1, layer)
                if layer == 0:
                    split_hi(1)
                for u, b, i in loops(act, layer):
                    for s in range(BODY):
                        if s in ((5, 8) if u is None else (0, 4, 8)):
                            blk = (2, 0, 1)[s // CHUNKS]
                            if u is None and s == 5:
                                act.wait_ge(S["pre_rdy"], layer + 1)
                            if u is not None and s == 0:
                                act.wait_ge(S["o_full"], u.head(0))
                            if u is not None and s > 0:
                                act.wait_ge(S["qk_full"], 4 * u.index + s // 2)
                            take(CHUNK0[layer] + BODY * (b + i) + s // CHUNKS * CHUNKS, blk, unit[:, blk, :, :])
                        if u is None and 1 <= 2 * s <= 6:
                            turned(16 * layer + 2 * s + 1, layer)
                        attention(u, 2 * s)
                        if u is None and 1 <= 2 * s + 1 <= 6:
                            turned(16 * layer + 2 * s + 2, layer)
                        split_hi(CHUNK0[layer] + BODY * b + s + 2, i)
                        attention(u, 2 * s + 1)
                        if layer == 0 and u is None and s == 10:
                            act.wait_ge(S["lam_s"], 1)
                            nc.scalar.activation(lame[:, :], lams[:, :], ACT.Exp).then_inc(S["lam_e"], 1)
                        if layer == 0 and u is None and s == 0:
                            for t in range(NT):
                                for n in range(2):
                                    act.dma_start(x_halves[t][n], x_nat[t * P:(t + 1) * P, n * 1024:(n + 1) * 1024]
                                                  ).then_inc(S["nat_in"], 16)
                        if u is None and s in (3, 4):
                            pre_squares(layer, s - 3)
                        if u is None and s == 4:
                            act.wait_ge(S["pre_var"], layer + 1)
                            nc.scalar.activation(std[:, :], var[:, :], ACT.Sqrt).then_inc(S["pre_std"], 1)
                g0 = CHUNK0[layer] + BODY * BODIES[layer]
                def out_squares(n, t, sem_done, count):
                    act.wait_ge(sem_done, count)
                    if t == 0:
                        act.wait_ge(S["y_sq"], NT * (OUT_BLOCKS * layer + n))
                    nc.scalar.activation(probs[:, t, :], acc[OUT_SET[n]][t][:, :], ACT.Square,
                                         accum_out=y_ss[:, t, n:n + 1]).then_inc(S["y_sq"], 1)

                def out_root(t):
                    act.wait_ge(S["y_var"], NT * layer + t + 1)
                    nc.scalar.activation(std[:, t:t + 1], var[:, t:t + 1], ACT.Sqrt).then_inc(S["y_std"], 1)

                for s in range(CHUNKS + len(OUT_ORDER)):
                    if s == 0:
                        act.wait_ge(S["o_full"], CREDIT + HEADS[layer])
                        take(g0, 2, unit[:, 2, :, :])
                        if layer == 0:
                            act.wait_ge(S["rs_v"], 1)
                            nc.scalar.activation(bstd[:, :], row_sum[:, 16:32], ACT.Sqrt).then_inc(S["rs_s"], 1)
                    if s == CHUNKS:
                        take(g0 + CHUNKS, 0, unit_out)
                    if s in OUT_SLOTS:
                        for t in range(NT):
                            out_squares(OUT_SLOTS.index(s), t, S["chunk_used"], g0 + s)
                    if s == LAST:
                        nc.scalar.activation(warm[:, :], pre_ss[:, 0, 0:1], ACT.Sqrt)
                        out_squares(OUT_BLOCKS - 1, 0, S["tile_done"], layer + 1)
                        out_root(0)
                    if s in TURN_SLOTS:
                        c = TURN_SLOTS.index(s)
                        turned(16 * layer + 8 + 2 * c, layer)
                        turned(16 * layer + 9 + 2 * c, layer)
                    if s in GATE_SLOTS:
                        c = GATE_SLOTS.index(s)
                        if c == 0:
                            act.wait_ge(S["unit_done"], CREDIT + UNITS[layer])
                        else:
                            act.wait_ge(S["gate_u"], CHUNKS * layer + c)
                        src = unit_out_flat if c == 3 else unit[:, c, :, :].rearrange("p t n -> p (t n)")
                        if c >= 2:
                            act.wait_ge(S["proj_ready"], PROJ0[layer] + 3 * BODIES[layer] + c - 2)
                        nc.scalar.activation(scores_flat, src, ACT.Tanh, scale=0.5).then_inc(S["tanh_done"], 1)
                    if s < CHUNKS + len(OUT_ORDER):
                        split_hi(g0 + s + 2)
                if layer == 0:
                    turned(16, 1)
                out_squares(OUT_BLOCKS - 1, 1, S["chunk_used"], g0 + LAST + 1)
                out_root(1)

        @block.vector
        def _(dve):
            def split_lo(at, i=0):
                if at >= ALL_CHUNKS:
                    return
                if at == 0:
                    for n, (sem_hi, sem_lo) in enumerate((("first_hi", "first_lo"), ("hi_ready", "lo_ready"))):
                        cols = slice(n * CK * NB // 2, (n + 1) * CK * NB // 2)
                        dve.wait_ge(S[sem_hi], 1)
                        nc.vector.tensor_tensor(w_lo[:, 0, cols], raw[:, 0, cols], w_hi[:, 0, cols].bitcast(F32),
                                                ALU.subtract).then_inc(S[sem_lo], 1)
                    return
                dve.wait_ge(S["hi_ready"], at + BODY * i + 1)
                nc.vector.tensor_tensor(w_lo[:, at % SPLIT, :], raw[:, at % RAW, :],
                                        w_hi[:, at % SPLIT, :].bitcast(F32), ALU.subtract).then_inc(S["lo_ready"], 1)

            def turned(f, layer):
                dve.wait_ge(S["turn_hi"], f + 1)
                if f < 8:
                    for kt in (2 * f, 2 * f + 1):
                        m = nc.vector.scalar_tensor_tensor(act_lo[:, kt, :], xT[:, kt, :], preg[:, 0, kt:kt + 1],
                                                           act_hi[:, kt, :].bitcast(F32), ALU.mult, ALU.subtract)
                    m.then_inc(S["turn_taken"], 1)
                    return
                if 16 <= f < 24:
                    c, t = START[f - 16]
                    tile = slice(t * P, (t + 1) * P)
                    for kk in range(CK):
                        kt = c * CK + kk
                        m = nc.vector.scalar_tensor_tensor(act_lo[:, kt, tile], bank[f % 2][:, kk * P:(kk + 1) * P],
                                                           preg[:, 1, kt:kt + 1], act_hi[:, kt, tile].bitcast(F32),
                                                           ALU.mult, ALU.subtract)
                    m.then_inc(S["turn_taken"], 1)
                    return
                for n in range(2):
                    kt = 2 * (f % 8) + n
                    src, hi, lo = bank[f % 2][:, n * SEQ:(n + 1) * SEQ], act_hi[:, kt, :].bitcast(F32), act_lo[:, kt, :]
                    if layer == 0:
                        m = nc.vector.tensor_tensor(lo.rearrange("p (c b a) -> p c b a", c=4, b=4),
                                                    src.rearrange("p (a b c) -> p c b a", b=4, c=4),
                                                    hi.rearrange("p (c b a) -> p c b a", c=4, b=4), ALU.subtract)
                    else:
                        m = nc.vector.tensor_tensor(lo, src, hi, ALU.subtract)
                m.then_inc(S["turn_taken"], 1)

            def take_qk(u, f):
                parts = qk_parts(u, f)
                if parts is None:
                    tile = unit_out_flat if u.kind == "D" else (g_qT, g_kT)[f // 2]
                    dve.wait_ge(S["qk_full"], 4 * u.index + f + 1)
                    nc.vector.tensor_copy(tile[:, f % 2 * NB:(f % 2 + 1) * NB], bank[f % 2][:, :]).then_inc(
                        S["qk_ready"], 1)
                    return
                hi, lo, n = parts
                before = 4 * u.index if u.kind != "D" else 4 * (u.index - 4)
                dve.wait_ge(S["qk_hi"], before + (3 if f == 4 else f + 1))
                if f == 4:
                    nc.vector.tensor_copy(late_k[:, :], bank[0][:, n:2 * n])
                nc.vector.tensor_tensor(lo, bank[f % 2][:, 0:n], hi.bitcast(F32), ALU.subtract).then_inc(S["qk_ready"], 1)

            def mask_and_max(u, j):
                w = P if u.kind == "G" else SEQ
                dve.wait_ge(S["s_full"], u.plain(j) + 1)
                if u.kind == "A" and j == 0:
                    dve.wait_ge(S["bias_rdy"], UH)
                dve.wait_ge(S["probs_ready"], u.head(j) - 1 if j else u.head(0))
                dst = scores[:, j % 2, 0:NT * w]
                if u.kind == "G":
                    for t in range(NT):
                        m = nc.vector.scalar_tensor_tensor(dst[:, t * P:(t + 1) * P], Y[:, t * P:(t + 1) * P], SCALE,
                                                           const(u.mask), ALU.mult, ALU.add)
                else:
                    if u.kind == "A":
                        add = bias_a[:, bass.ds((UH * u.step + j) * NT * SEQ, NT * SEQ)]
                    else:
                        add = const(u.mask)
                    m = nc.vector.scalar_tensor_tensor(dst, Y[:, :], SCALE, add, ALU.mult, ALU.add)
                m.then_inc(S["masked"], 1)
                two = slice(2 * j, 2 * j + 2)
                dve.wait_ge(S["masked"], u.plain(j) + 1)
                nc.vector.reduce_max(rmax[:, two], dst.rearrange("p (t n) -> p t n", t=NT), AX_X).then_inc(S["maxed"], 1)
                dve.wait_ge(S["maxed"], u.plain(j) + 1)
                if u.kind == "D":
                    nc.vector.tensor_scalar(negm[:, two], rmax[:, two], -1.0, negsink[:, j:j + 1], ALU.mult,
                                            ALU.min).then_inc(S["negm_ready"], 1)
                else:
                    nc.vector.tensor_scalar(negm[:, two], rmax[:, two], -1.0, None, ALU.mult).then_inc(S["negm_ready"], 1)

            def max_map(u, j, c):
                dve.wait_ge(S[f"map{c}_full"], u.diff(j) + 1)
                nc.vector.reduce_max(bmax[:, c, :], bank[1 - c][:, :].rearrange("p (t n) -> p t n", t=NT),
                                     AX_X).then_inc(S[f"map{c}_max"], 1)
                dve.wait_ge(S[f"map{c}_max"], u.diff(j) + 1)
                nc.vector.tensor_scalar(bneg[:, c, :], bmax[:, c, :], -SCALE_B, None, ALU.mult).then_inc(
                    S[f"map{c}_neg"], 1)

            def combine(u, j):
                n = u.diff(j)
                dve.wait_ge(S["map0_exp"], n + 1)
                dve.wait_ge(S["map1_exp"], n + 1)
                nc.vector.reciprocal(binv[:, :, :], bsum[:, :, :]).then_inc(S["b_inv"], 1)
                dve.wait_ge(S["b_inv"], n + 1)
                nc.vector.tensor_scalar(bw[:, :], binv[:, 1, :], neglam[:, 0:1], None, ALU.mult).then_inc(S["b_w"], 1)
                for t in range(NT):
                    sl = slice(t * SEQ, (t + 1) * SEQ)
                    m = nc.vector.tensor_scalar(scores[:, 0, sl], scores[:, 0, sl], binv[:, 0, t:t + 1], None, ALU.mult)
                m.then_inc(S["b_scaled"], 1)
                dve.wait_ge(S["b_w"], n + 1)
                dve.wait_ge(S["b_scaled"], n + 1)
                dve.wait_ge(S["pt_full"], u.head(j) - 1 if j else u.head(0))
                for t in range(NT):
                    sl = slice(t * SEQ, (t + 1) * SEQ)
                    m = nc.vector.scalar_tensor_tensor(probs[:, j % 2, sl], scores[:, 1, sl], bw[:, t:t + 1],
                                                       scores[:, 0, sl], ALU.mult, ALU.add)
                m.then_inc(S["probs_ready"], 1)

            def take_pT(u, j):
                dve.wait_ge(S["pt_full"], u.head(j) + 1)
                dve.wait_ge(S["o_full"], u.head(j))
                n = SEQ if u.kind == "G" else 2 * SEQ
                nc.vector.tensor_copy(pT[:, 0:n], X[:, 0:n]).then_inc(S["pt_ready"], 1)

            def take_out(u, j):
                dve.wait_ge(S["o_full"], u.head(j) + 1)
                src = X[:, 0:NT * HEAD].rearrange("p (t d) -> p t d", t=NT)
                if u.kind == "G":
                    dst = unit_out[:, :, j * HEAD:(j + 1) * HEAD]
                elif u.kind == "D":
                    dst = mix[:, :, 2 * NB + j * HEAD:2 * NB + (j + 1) * HEAD]
                elif u.kind == "W":
                    dst = mix[:, :, bass.ds(NB * u.step + j * HEAD, HEAD)]
                else:
                    dst = mix[:, :, bass.ds(NB * u.index + j * HEAD, HEAD)]
                if u.kind == "B":
                    dve.wait_ge(S["o_squared"], CREDIT + u.diff(j) + 1)
                    weights_of_d = subg[:, :].unsqueeze(1).to_broadcast([P, NT, HEAD])
                    nc.vector.tensor_tensor(dst, src, weights_of_d, ALU.mult).then_inc(S["o_taken"], 1)
                else:
                    nc.vector.tensor_scalar(dst, src, 1.0, None, ALU.mult).then_inc(S["o_taken"], 1)

            def close(u):
                if u.kind in ("A", "B"):
                    nc.vector.tensor_scalar(row_sum[:, bass.ds(8 * u.index, 8)], usum[:, 0:8], 1.0, None,
                                            ALU.mult).then_inc(S["unit_done"], 1)
                elif u.kind == "W":
                    nc.vector.tensor_scalar(row_sum[:, bass.ds(8 * u.step, 8)], usum[:, 0:8], 1.0, None, ALU.mult)
                    nc.vector.tensor_scalar(cneg[:, bass.ds(u.step, 1), :], negm[:, 0:8].rearrange("p (a n) -> p a n", a=1),
                                            1.0, None, ALU.mult).then_inc(S["unit_done"], 1)
                elif u.kind == "D":
                    dve.wait_ge(S["sink_ready"], 8)
                    nc.vector.tensor_tensor(row_sum[:, 16:32], usum[:, :], sinke[:, :], ALU.add).then_inc(S["unit_done"], 1)
                else:
                    n = u.index - 6
                    old_neg = cneg[:, bass.ds(u.step, 1), :].rearrange("p a n -> p (a n)")
                    total = row_sum[:, bass.ds(8 * u.step, 8)]
                    nc.vector.tensor_tensor(newneg[:, :], old_neg, negm[:, 0:8], ALU.min).then_inc(S["m_new"], 1)
                    dve.wait_ge(S["m_new"], n + 1)
                    nc.vector.tensor_tensor(dexp[:, 0, :], newneg[:, :], old_neg, ALU.subtract)
                    nc.vector.tensor_tensor(dexp[:, 1, :], newneg[:, :], negm[:, 0:8], ALU.subtract).then_inc(S["m_diff"], 1)
                    dve.wait_ge(S["m_diff"], n + 1)
                    nc.vector.tensor_scalar(old_neg, newneg[:, :], 1.0, None, ALU.mult)
                    dve.wait_ge(S["m_exp"], n + 1)
                    nc.vector.tensor_tensor(wsum[:, :], usum[:, 0:8], wexp[:, 1, :], ALU.mult)
                    nc.vector.tensor_tensor(total, total, wexp[:, 0, :], ALU.mult).then_inc(S["m_wsum"], 1)
                    dve.wait_ge(S["o_taken"], u.head(UH))
                    for t in range(NT):
                        old = mix[:, t, bass.ds(NB * u.step, NB)].rearrange("p (h d) -> p h d", h=UH)
                        new = unit_out[:, t, :].rearrange("p (h d) -> p h d", h=UH)
                        w = [wexp[:, k, :].rearrange("p (h t) -> p t h", t=NT)[:, t, :].unsqueeze(2).to_broadcast([P, UH, HEAD])
                             for k in range(2)]
                        nc.vector.tensor_tensor(old, old, w[0], ALU.mult)
                        m = nc.vector.tensor_tensor(new, new, w[1], ALU.mult)
                    m.then_inc(S["m_scaled"], 1)
                    dve.wait_ge(S["m_wsum"], n + 1)
                    nc.vector.tensor_tensor(total, total, wsum[:, :], ALU.add)
                    dve.wait_ge(S["m_scaled"], n + 1)
                    for t in range(NT):
                        old = mix[:, t, bass.ds(NB * u.step, NB)]
                        m = nc.vector.tensor_tensor(old, old, unit_out[:, t, :], ALU.add)
                    m.then_inc(S["unit_done"], 1)

            def attention(u, h):
                if u is None:
                    return
                for f in u.fills(h):
                    take_qk(u, f)
                for j in u.stages(h, 4):
                    take_out(u, j)
                if u.kind == "B":
                    for j in u.stages(h, 0):
                        max_map(u, j, 0)
                    for j in u.stages(h, 1):
                        max_map(u, j, 1)
                    for j in u.stages(h, 2):
                        combine(u, j)
                else:
                    for j in u.stages(h, 0):
                        mask_and_max(u, j)
                for j in u.stages(h, 3):
                    take_pT(u, j)
                if h == 2 * BODY - 1:
                    close(u)

            def gate(layer, c):
                n = CHUNKS * layer + c
                src = unit_out_flat if c == 3 else unit[:, c, :, :].rearrange("p t n -> p (t n)")
                dve.wait_ge(S["tanh_done"], n + 1)
                if n:
                    dve.wait_ge(S["gate_done"], n)
                nc.vector.scalar_tensor_tensor(probs_flat, scores_flat, 1.0, src, ALU.add, ALU.mult).then_inc(S["gate_u"], 1)
                dve.wait_ge(S["gate_u"], n + 1)
                if (layer, c) in RS_WAITS:
                    dve.wait_ge(S["rs_rdy"], RS_WAITS[layer, c])
                for t in range(NT):
                    for hh in range(UH):
                        o = mix[:, t, c * NB + hh * HEAD:c * NB + (hh + 1) * HEAD]
                        k = 8 * c + 2 * hh + t
                        m = nc.vector.scalar_tensor_tensor(o, o, row_scale[:, k:k + 1],
                                                           probs[:, t, hh * HEAD:(hh + 1) * HEAD], ALU.mult, ALU.mult)
                m.then_inc(S["gate_done"], 1)

            def scale_out(layer, n, t):
                dve.wait_ge(S["y_sq"], NT * (OUT_BLOCKS * layer + n) + t + 1)
                return nc.vector.tensor_tensor(mix[:, t, n * NB:(n + 1) * NB], acc[OUT_SET[n]][t][:, :],
                                               postg[:, n * NB:(n + 1) * NB], ALU.mult)

            def post_norm(layer, t):
                count, one = NT * layer + t + 1, slice(t, t + 1)
                dve.wait_ge(S["y_sq"], NT * (OUT_BLOCKS * layer + OUT_BLOCKS - 1) + t + 1)
                nc.vector.reduce_sum(ss[:, one], y_ss[:, t, :], AX_X).then_inc(S["y_sum"], 1)
                dve.wait_ge(S["y_sum"], count)
                nc.vector.tensor_scalar(var[:, one], ss[:, one], 1.0 / D_MODEL, EPS, ALU.mult,
                                        ALU.add).then_inc(S["y_var"], 1)
                m = scale_out(layer, OUT_BLOCKS - 1, t)
                if t == NT - 1:
                    m.then_inc(S["y_scaled"], 1)
                dve.wait_ge(S["y_std"], count)
                nc.vector.reciprocal(post_r[:, one], std[:, one]).then_inc(S["y_rdy"], 1)

            def new_x(layer, t, blocks):
                dve.wait_ge(S["y_rdy"], NT * layer + t + 1)
                if layer == 0:
                    dve.wait_ge(S["resid_in"], 16 * NT)
                for n in blocks:
                    cols = slice(n * NB, (n + 1) * NB)
                    nc.vector.scalar_tensor_tensor(resid[:, t, cols], mix[:, t, cols], post_r[:, t:t + 1],
                                                   resid[:, t, cols], ALU.mult, ALU.add).then_inc(x_new[t], 1)

            def small_things():
                dve.wait_ge(S["vecs_in"], 16 * 3)
                lv = lamv[:, :, :].rearrange("p (a b) n -> p a b n", a=2)
                nc.vector.tensor_tensor(lamp[:, :, :], lv[:, :, 0, :], lv[:, :, 1, :], ALU.mult).then_inc(S["lam_p"], 1)
                dve.wait_ge(S["lam_p"], 1)
                nc.vector.reduce_sum(lams[:, :], lamp[:, :, :], AX_X).then_inc(S["lam_s"], 1)
                nc.vector.tensor_scalar(negsink[:, :], sinkb[:, :], -1.0, None, ALU.mult)
                dve.wait_ge(S["lam_e"], 1)
                nc.vector.scalar_tensor_tensor(neglam[:, :], lame[:, 1:2], -LAMBDA_INIT, lame[:, 0:1], ALU.add,
                                               ALU.subtract)

            turned(0, 0)
            for layer in range(2):
                if layer == 0:
                    split_lo(0)
                turned(16 * layer + 1, layer)
                if layer == 0:
                    split_lo(1)
                else:
                    new_x(0, 1, (2, 3))
                for u, b, i in loops(dve, layer):
                    for s in range(BODY):
                        if u is None and 1 <= 2 * s <= 6:
                            turned(16 * layer + 2 * s + 1, layer)
                        attention(u, 2 * s)
                        if u is None and s == 5:
                            dve.wait_ge(S["pre_sq"], 2 * layer + 2)
                            nc.vector.reduce_sum(ss[:, :], pre_ss[:, :, 0:2], AX_X).then_inc(S["pre_sum"], 1)
                            dve.wait_ge(S["pre_sum"], layer + 1)
                            nc.vector.tensor_scalar(var[:, :], ss[:, :], 1.0 / D_MODEL, EPS, ALU.mult,
                                                    ALU.add).then_inc(S["pre_var"], 1)
                        if u is not None and u.kind != "D":
                            attention(u, 2 * s + 1)
                        if u is None and s == 5:
                            dve.wait_ge(S["pre_std"], layer + 1)
                            nc.vector.reciprocal(pre_r[:, :], std[:, :]).then_inc(S["pre_rdy"], 1)
                        if u is None and 1 <= 2 * s + 1 <= 6:
                            turned(16 * layer + 2 * s + 2, layer)
                        split_lo(CHUNK0[layer] + BODY * b + s + 2, i)
                        if u is not None and u.kind == "D":
                            attention(u, 2 * s + 1)
                        if layer == 0 and u is None and s == 10:
                            small_things()
                        if layer == 0 and u is None and s >= BODY - UH:
                            pair = s - (BODY - UH)
                            dve.wait_ge(bias_in_two[pair], 16 * 2 * 2 * NT)
                            dve.wait_ge(S["consts_in"], 16)
                            for g in range(2 * NT * pair, 2 * NT * (pair + 1)):
                                turned_keys, keys = (v[:, g * SEQ:(g + 1) * SEQ].rearrange("p (j k) -> p j k", j=ROWS)
                                                     for v in (bias_in, bias_a))
                                mask = const("mask_a").rearrange("p (j k) -> p j k", j=ROWS)
                                m = nc.vector.tensor_tensor(keys, turned_keys[:, :, ::-1], mask, ALU.add)
                            m.then_inc(S["bias_rdy"], 1)
                g0 = CHUNK0[layer] + BODY * BODIES[layer]
                for s in range(CHUNKS + len(OUT_ORDER)):
                    if s == 0:
                        dve.wait_ge(S["unit_done"], CREDIT + UNITS[layer])
                        n = 16 if layer == 0 else 32
                        m = nc.vector.tensor_scalar(row_sum[:, 0:n], row_sum[:, 0:n], 2.0, None, ALU.mult)
                        if layer == 0:
                            up = (0.5 * (1.0 - LAMBDA_INIT)) ** -2
                            m = nc.vector.tensor_scalar(row_sum[:, 16:32], row_sum[:, 16:32], up / HEAD, up * EPS,
                                                        ALU.mult, ALU.add)
                        m.then_inc(S["rs_v"], 1)
                        dve.wait_ge(S["rs_v"], layer + 1)
                        nc.vector.reciprocal(row_scale[:, 0:n], row_sum[:, 0:n]).then_inc(S["rs_rdy"], 1)
                    if s == 2 and layer == 0:
                        dve.wait_ge(S["rs_s"], 1)
                        nc.vector.reciprocal(row_scale[:, 16:32], bstd[:, :]).then_inc(S["rs_rdy"], 1)
                    if s in OUT_SLOTS:
                        n = OUT_SLOTS.index(s)
                        if n == 0:
                            dve.wait_ge(S["postg_in"], 16 * (layer + 1))
                        for t in range(NT):
                            m = scale_out(layer, n, t)
                        m.then_inc(S["y_scaled"], 1)
                    if s == LAST:
                        post_norm(layer, 0)
                        new_x(layer, 0, range(OUT_BLOCKS))
                    if s in TURN_SLOTS:
                        c = TURN_SLOTS.index(s)
                        turned(16 * layer + 8 + 2 * c, layer)
                        turned(16 * layer + 9 + 2 * c, layer)
                    if s in GATE_SLOTS:
                        gate(layer, GATE_SLOTS.index(s))
                    if s < CHUNKS + len(OUT_ORDER):
                        split_lo(g0 + s + 2)
                if layer == 0:
                    turned(16, 1)
                post_norm(layer, 1)
                new_x(layer, 1, (0, 1) if layer == 0 else range(OUT_BLOCKS))


def constants():
    f = np.float32
    p = np.arange(P)
    made = {}
    col, key = p % GRID_W, np.arange(SEQ) % GRID_W
    start = np.clip(col - 8, 0, GRID_W - 16)
    ok = (key[None] >= start[:, None]) & (key[None] < start[:, None] + 16)
    made["mask_a"] = np.where(ok, f(0), f(NEG))
    tok = token_order()

    def window(half):
        q = tok.reshape(NT, P).T
        ok = np.abs(q[:, :, None] - tok[None, None]) <= half
        return np.where(ok, f(0), f(NEG)).reshape(P, NT * SEQ)

    made["mask_w"], made["mask_d"] = window(64), window(128)
    for name, n in (("mask_g1", 64), ("mask_g2", 16)):
        made[name] = np.where(p[:, None] // n == p[None] // n, f(0), f(NEG))
    for layer, (half, order) in enumerate(((8, np.arange(SEQ)), (16, tok))):
        inv = f(500000.0) ** (-np.arange(half, dtype=f) / f(half))
        ang = order.astype(f)[:, None] * inv.astype(f)[None]
        cos, sin = np.cos(ang).astype(f), np.sin(ang).astype(f)
        for name, tab in (("cos", [cos, cos]), ("sin", [-sin, sin])):
            made[f"{name}{layer}"] = np.concatenate(tab, 1).reshape(NT, P, 2 * half).transpose(1, 0, 2).reshape(P, -1)
    return np.ascontiguousarray(np.concatenate([made[n].astype(f) for n in CONST_COLS], 1))


def token_order():
    return np.arange(SEQ).reshape(16, 4, 4).transpose(2, 1, 0).reshape(-1)


def in_blocks():
    a = [[base + 512 * u for base in (0, 1024, 2048)] for u in range(2)]
    b = [[base + 512 * u for base in (4096, 5120, 6144)] for u in range(2)]
    first = sum(a + b, []) + [3072, 3584, 7168, 7680]
    c = [[base + 1024 * g + 512 * u for base in (0, 3072, 6144)] for g in range(3) for u in range(2)]
    second = sum(c, []) + [10240, 10752, 11264] + [9216, 9728, 11776, 12288]
    return first, second


def pack_weights(w_ins, w_outs):
    packed = np.empty((ALL_CHUNKS, P, CK, NB), np.float32)
    g = 0
    for w_in, w_out, starts in zip(w_ins, w_outs, in_blocks()):
        places = [(w_in, s, c) for s in starts for c in range(CHUNKS)]
        places += [(w_out, n * NB, c) for n, c in OUT_ORDER]
        for w, s, c in places:
            packed[g] = w[c * CK * P:(c + 1) * CK * P, s:s + NB].reshape(CK, P, NB).transpose(1, 0, 2)
            g += 1
    return packed.reshape(ALL_CHUNKS, P, CK * NB)


def kernel(**inputs):
    import concourse.bacc as _bacc
    from concourse.bass_utils import run_bass_kernel_spmd as _run

    x = {k: np.asarray(v) for k, v in inputs.items()}
    order = token_order()
    rows = x["x"].reshape(SEQ, D_MODEL)
    per_k = lambda g: g.reshape(KT, P).T
    arrays = {
        "weights": pack_weights((x["l0_w_in"], x["l1_w_in"]), (x["l0_w_out"], x["l1_w_out"])),
        "x_turned": rows.T.reshape(KT, P, SEQ).transpose(1, 0, 2),
        "x_nat": rows,
        "x_perm": rows[order],
        "consts": constants(),
        "identity": np.eye(P, dtype=np.float32),
        "pre_g": np.stack([per_k(x["l0_pre_g"]), per_k(x["l1_pre_g"])], 1),
        "post_g": np.stack([x["l0_post_g"], x["l1_post_g"]]),
        "rpb": x["l0_rpb"][:, :, ::-1].reshape(-1),
        "lam": np.concatenate([x["l0_lam_q1"], x["l0_lam_k1"], x["l0_lam_q2"], x["l0_lam_k2"]]),
        "subln": x["l0_subln_g"],
        "sink": x["l1_sink"],
    }
    arrays = {k: np.ascontiguousarray(v) for k, v in arrays.items()}
    nc = _bacc.Bacc("TRN2", target_bir_lowering=False, num_devices=1)
    args = [nc.dram_tensor(k, v.shape, mybir.dt.from_np(v.dtype), kind="ExternalInput").ap() for k, v in arrays.items()]
    out = nc.dram_tensor("out_0", (SEQ, D_MODEL), F32, kind="ExternalOutput").ap()
    build(nc, *args, out)
    r = _run(nc, [arrays], core_ids=[0])
    got = np.empty((SEQ, D_MODEL), np.float32)
    got[order] = r.results[0]["out_0"]
    return got.reshape(1, SEQ, D_MODEL)
```
